# Optimizing a Trainium2 kernel written in Bass

```python
import jax
import jax.numpy as jnp
from jax import lax
import numpy as np

D_MODEL = 1024
BATCH = 1
SEQ = 512
DEPTH = 2

GRID_W = 64
CTX_LEN = 256
EPS = 1e-6
N_MOD = 6
A_GROUPS = 4
A_GROUP_DIM = 128
A_WIDTH = A_GROUPS * A_GROUP_DIM
CHUNK = 128
N_Q_HEADS = 4
N_KV_HEADS = 2
HEAD_DIM = 128
Q_BLOCK = 128
ROPE_THETA = 10000.0
B_WIDTH = N_Q_HEADS * HEAD_DIM
KV_WIDTH = N_KV_HEADS * HEAD_DIM
AB_IN = 2 * A_WIDTH + B_WIDTH + 2 * KV_WIDTH
AB_OUT = A_WIDTH + B_WIDTH
D_RNN = 1280
RNN_BLOCK = 128
N_RNN_BLOCKS = D_RNN // RNN_BLOCK
CONV_W = 4
RG_C = 8.0
PEER_HEADS = 8
N_KEYS = 128
N_EXPERTS = N_KEYS * N_KEYS
PEER_TOPK = 16
D_KEY = 256
TOKEN_BLOCK = 128
N_EVEN = (DEPTH + 1) // 2
N_ODD = DEPTH // 2

kernel_name = 'hybrid_gmlp_gqa_rglru_peer_trunk'

def rmsnorm(x, g):
    xf = x.astype(jnp.float32)
    y = xf * lax.rsqrt(jnp.mean(xf * xf, axis=-1, keepdims=True) + EPS)
    return y.astype(x.dtype) * g

def modulate(h, shift, scale):
    return h * (1 + scale) + shift

def axial_rope_tables(rows):
    n = rows * GRID_W
    row = jnp.broadcast_to(jnp.arange(rows, dtype=jnp.int32)[:, None], (rows, GRID_W)).reshape(n)
    col = jnp.broadcast_to(jnp.arange(GRID_W, dtype=jnp.int32)[None, :], (rows, GRID_W)).reshape(n)
    n_freq = HEAD_DIM // 4
    inv_freq = ROPE_THETA ** (-jnp.arange(n_freq, dtype=jnp.float32) / n_freq)
    ang = jnp.stack([row.astype(jnp.float32)[:, None] * inv_freq,
                     col.astype(jnp.float32)[:, None] * inv_freq], axis=1)
    return jnp.cos(ang), jnp.sin(ang)

def apply_axial_rope(x, cos, sin):
    b, n, h, d = x.shape
    xf = x.astype(jnp.float32).reshape(b, n, h, 2, 2, d // 4)
    c = cos[None, :, None]
    s = sin[None, :, None]
    x1, x2 = xf[..., 0, :], xf[..., 1, :]
    out = jnp.stack([x1 * c - x2 * s, x2 * c + x1 * s], axis=-2)
    return out.reshape(b, n, h, d).astype(x.dtype)

def block_attention(q, k, v):
    b, n, h, d = q.shape
    g = h // N_KV_HEADS
    qb = q.reshape(b, n // Q_BLOCK, Q_BLOCK, N_KV_HEADS, g, d).transpose(1, 0, 2, 3, 4, 5)
    scale = HEAD_DIM ** -0.5

    def one_block(qblk):
        s = jnp.einsum('bqkgd,bmkd->bkgqm', qblk, k).astype(jnp.float32) * scale
        p = jax.nn.softmax(s, axis=-1).astype(v.dtype)
        return jnp.einsum('bkgqm,bmkd->bqkgd', p, v)

    o = lax.map(one_block, qb)
    return o.transpose(1, 0, 2, 3, 4, 5).reshape(b, n, h * d)

def chunk_gmlp(za, norm_g, ws, bs):
    b, n, _ = za.shape
    za = jax.nn.gelu(za)
    u, vv = za[..., :A_WIDTH], za[..., A_WIDTH:]
    vv = rmsnorm(vv.reshape(b, n, A_GROUPS, A_GROUP_DIM), norm_g.reshape(A_GROUPS, A_GROUP_DIM))
    vv = vv.reshape(b, n // CHUNK, CHUNK, A_GROUPS, A_GROUP_DIM)
    s = jnp.einsum('gpq,bnqgc->bnpgc', ws, vv) + bs.T[None, None, :, :, None]
    return u * s.reshape(b, n, A_WIDTH)

def split_ab(z):
    b, n, _ = z.shape
    o1 = 2 * A_WIDTH
    o2 = o1 + B_WIDTH
    o3 = o2 + KV_WIDTH
    za = z[..., :o1]
    q = z[..., o1:o2].reshape(b, n, N_Q_HEADS, HEAD_DIM)
    k = z[..., o2:o3].reshape(b, n, N_KV_HEADS, HEAD_DIM)
    v = z[..., o3:].reshape(b, n, N_KV_HEADS, HEAD_DIM)
    return za, q, k, v

def mixer_ab(h, hc, cos, sin, w_in, gm_g, ws, bs, qg, kg, w_out, need_ctx):
    za, q, k, v = split_ab(h @ w_in)
    zac, qc, kc, vc = split_ab(hc @ w_in)
    q = apply_axial_rope(rmsnorm(q, qg), cos, sin)
    k = apply_axial_rope(rmsnorm(k, kg), cos, sin)
    kc = rmsnorm(kc, kg)
    k_all = jnp.concatenate([kc, k], axis=1)
    v_all = jnp.concatenate([vc, v], axis=1)
    y = jnp.concatenate([chunk_gmlp(za, gm_g, ws, bs), block_attention(q, k_all, v_all)], axis=-1) @ w_out
    if not need_ctx:
        return y, None
    qc = rmsnorm(qc, qg)
    yc = jnp.concatenate([chunk_gmlp(zac, gm_g, ws, bs), block_attention(qc, kc, vc)], axis=-1) @ w_out
    return y, yc

def centred_dwconv(x, w, b):
    y = lax.conv_general_dilated(
        x, w[:, None, :], window_strides=(1,),
        padding=[(CONV_W // 2, CONV_W - 1 - CONV_W // 2)],
        dimension_numbers=('NWC', 'WIO', 'NWC'),
        feature_group_count=x.shape[-1])
    return y + b

def linear_combine(e1, e2):
    a1, b1 = e1
    a2, b2 = e2
    return a1 * a2, a2 * b1 + b2

def rglru_coeffs(xr, wa, ba, wx, bx, lam):
    b, n, _ = xr.shape
    xb = xr.reshape(b, n, N_RNN_BLOCKS, RNN_BLOCK)
    r = jax.nn.sigmoid(jnp.einsum('bnhi,hij->bnhj', xb, wa).reshape(b, n, D_RNN) + ba)
    i = jax.nn.sigmoid(jnp.einsum('bnhi,hij->bnhj', xb, wx).reshape(b, n, D_RNN) + bx)
    log_a = -RG_C * r.astype(jnp.float32) * jax.nn.softplus(-lam.astype(jnp.float32))
    u = jnp.sqrt(-jnp.expm1(2.0 * log_a)) * (i * xr).astype(jnp.float32)
    return jnp.exp(log_a), u

def mixer_rglru(h, hc, w_in, conv_w, conv_b, wa, ba, wx, bx, lam, w_out, need_ctx):
    z = h @ w_in
    zc = hc @ w_in
    gate, xr = z[..., :D_RNN], z[..., D_RNN:]
    gate_c, xr_c = zc[..., :D_RNN], zc[..., D_RNN:]
    xr = centred_dwconv(xr, conv_w, conv_b)
    xr_c = centred_dwconv(xr_c, conv_w, conv_b)
    lat_states = []
    ctx_states = []
    for d in range(2):
        rev = d == 1
        ac, uc = rglru_coeffs(xr_c, wa[d], ba[d], wx[d], bx[d], lam[d])
        _, hc_seq = lax.associative_scan(linear_combine, (ac, uc), reverse=rev, axis=1)
        h_end = hc_seq[:, 0] if rev else hc_seq[:, -1]
        al, ul = rglru_coeffs(xr, wa[d], ba[d], wx[d], bx[d], lam[d])
        a_pre, h_seq = lax.associative_scan(linear_combine, (al, ul), reverse=rev, axis=1)
        lat_states.append(h_seq + a_pre * h_end[:, None, :])
        ctx_states.append(hc_seq)
    y_rec = (lat_states[0] + lat_states[1]).astype(h.dtype)
    y = (jax.nn.gelu(gate) * y_rec) @ w_out
    if not need_ctx:
        return y, None
    yc_rec = (ctx_states[0] + ctx_states[1]).astype(hc.dtype)
    yc = (jax.nn.gelu(gate_c) * yc_rec) @ w_out
    return y, yc

def peer_ffn(h, wq, keys, u_tab, v_tab):
    b, n, d = h.shape
    t = h.reshape(-1, TOKEN_BLOCK, d)

    def one_block(tb):
        q = (tb @ wq).reshape(TOKEN_BLOCK, PEER_HEADS, 2, D_KEY // 2)
        s = jnp.einsum('thsd,hskd->thsk', q, keys)
        v_half, i_half = lax.top_k(s, PEER_TOPK)
        cand = v_half[:, :, 0, :, None] + v_half[:, :, 1, None, :]
        cand_idx = i_half[:, :, 0, :, None] * N_KEYS + i_half[:, :, 1, None, :]
        top_s, pos = lax.top_k(cand.reshape(TOKEN_BLOCK, PEER_HEADS, PEER_TOPK * PEER_TOPK), PEER_TOPK)
        eidx = jnp.take_along_axis(cand_idx.reshape(TOKEN_BLOCK, PEER_HEADS, PEER_TOPK * PEER_TOPK), pos, axis=-1)
        gate = jax.nn.softmax(top_s.astype(jnp.float32), axis=-1).astype(tb.dtype)
        eidx = eidx.reshape(TOKEN_BLOCK, PEER_HEADS * PEER_TOPK)
        gate = gate.reshape(TOKEN_BLOCK, PEER_HEADS * PEER_TOPK)
        ue = jnp.take(u_tab, eidx, axis=0)
        ve = jnp.take(v_tab, eidx, axis=0)
        act = jax.nn.gelu(jnp.einsum('td,ted->te', tb, ue)) * gate
        return jnp.einsum('te,ted->td', act, ve)

    return lax.map(one_block, t).reshape(b, n, d)

def setup_inputs(seed: int = 0) -> dict:
    key = jax.random.key(seed)
    ks = jax.random.split(key, 32)
    D = D_MODEL

    def nrm(k, shape, scale):
        return jax.random.normal(k, shape, jnp.float32) * scale

    def gain(k, shape):
        return 1.0 + nrm(k, shape, 0.05)

    a0 = jax.random.uniform(ks[22], (N_ODD, 2, D_RNN), jnp.float32, minval=0.9, maxval=0.999)
    a_base = a0 ** (1.0 / RG_C)
    rg_lambda = jnp.log(a_base) - jnp.log1p(-a_base)
    return {
        'x': nrm(ks[0], (BATCH, SEQ, D), 1.0),
        'c': nrm(ks[1], (BATCH, D), 1.0),
        'ctx': nrm(ks[2], (BATCH, CTX_LEN, D), 1.0),
        'c_ctx': nrm(ks[3], (D,), 1.0),
        'mod_w': nrm(ks[4], (DEPTH, D, N_MOD * D), 0.5 * D ** -0.5),
        'mod_b': nrm(ks[5], (DEPTH, N_MOD * D), 0.02),
        'norm1_g': gain(ks[6], (DEPTH, D)),
        'norm2_g': gain(ks[7], (DEPTH, D)),
        'ab_w_in': nrm(ks[8], (N_EVEN, D, AB_IN), D ** -0.5),
        'gmlp_norm_g': gain(ks[9], (N_EVEN, A_WIDTH)),
        'gmlp_ws': nrm(ks[10], (N_EVEN, A_GROUPS, CHUNK, CHUNK), CHUNK ** -0.5),
        'gmlp_bs': gain(ks[11], (N_EVEN, A_GROUPS, CHUNK)),
        'q_norm_g': gain(ks[12], (N_EVEN, HEAD_DIM)),
        'k_norm_g': gain(ks[13], (N_EVEN, HEAD_DIM)),
        'ab_w_out': nrm(ks[14], (N_EVEN, AB_OUT, D), AB_OUT ** -0.5),
        'rg_w_in': nrm(ks[15], (N_ODD, D, 2 * D_RNN), D ** -0.5),
        'rg_conv_w': nrm(ks[16], (N_ODD, CONV_W, D_RNN), CONV_W ** -0.5),
        'rg_conv_b': nrm(ks[17], (N_ODD, D_RNN), 0.02),
        'rg_wa': nrm(ks[18], (N_ODD, 2, N_RNN_BLOCKS, RNN_BLOCK, RNN_BLOCK), RNN_BLOCK ** -0.5),
        'rg_ba': nrm(ks[19], (N_ODD, 2, D_RNN), 0.02),
        'rg_wx': nrm(ks[20], (N_ODD, 2, N_RNN_BLOCKS, RNN_BLOCK, RNN_BLOCK), RNN_BLOCK ** -0.5),
        'rg_bx': nrm(ks[21], (N_ODD, 2, D_RNN), 0.02),
        'rg_lambda': rg_lambda,
        'rg_w_out': nrm(ks[23], (N_ODD, D_RNN, D), D_RNN ** -0.5),
        'peer_wq': nrm(ks[24], (DEPTH, D, PEER_HEADS * D_KEY), D ** -0.5),
        'peer_keys': nrm(ks[25], (DEPTH, PEER_HEADS, 2, N_KEYS, D_KEY // 2), (D_KEY // 2) ** -0.5),
        'peer_u': nrm(ks[26], (DEPTH, N_EXPERTS, D), D ** -0.5),
        'peer_v': nrm(ks[27], (DEPTH, N_EXPERTS, D), 1.0),
        'final_norm_g': gain(ks[28], (D,)),
    }

def reference(x, c, ctx, c_ctx, mod_w, mod_b, norm1_g, norm2_g, ab_w_in, gmlp_norm_g, gmlp_ws, gmlp_bs,
              q_norm_g, k_norm_g, ab_w_out, rg_w_in, rg_conv_w, rg_conv_b, rg_wa, rg_ba, rg_wx, rg_bx,
              rg_lambda, rg_w_out, peer_wq, peer_keys, peer_u, peer_v, final_norm_g):
    n = x.shape[1]
    rows = n // GRID_W
    cos, sin = axial_rope_tables(rows)
    silu_c = jax.nn.silu(c)
    silu_cc = jax.nn.silu(c_ctx)
    for layer in range(DEPTH):
        last = layer == DEPTH - 1
        j = layer // 2
        mod = (silu_c @ mod_w[layer] + mod_b[layer])[:, None, :]
        modc = silu_cc @ mod_w[layer] + mod_b[layer]
        sh1, sc1, g1, sh2, sc2, g2 = jnp.split(mod, N_MOD, axis=-1)
        sh1c, sc1c, g1c, sh2c, sc2c, g2c = jnp.split(modc, N_MOD, axis=-1)
        h = modulate(rmsnorm(x, norm1_g[layer]), sh1, sc1)
        hc = modulate(rmsnorm(ctx, norm1_g[layer]), sh1c, sc1c)
        if layer % 2 == 0:
            y, yc = mixer_ab(h, hc, cos, sin, ab_w_in[j], gmlp_norm_g[j], gmlp_ws[j], gmlp_bs[j],
                             q_norm_g[j], k_norm_g[j], ab_w_out[j], not last)
        else:
            y, yc = mixer_rglru(h, hc, rg_w_in[j], rg_conv_w[j], rg_conv_b[j], rg_wa[j], rg_ba[j],
                                rg_wx[j], rg_bx[j], rg_lambda[j], rg_w_out[j], not last)
        x = x + g1 * y
        x = x + g2 * peer_ffn(modulate(rmsnorm(x, norm2_g[layer]), sh2, sc2),
                              peer_wq[layer], peer_keys[layer], peer_u[layer], peer_v[layer])
        if not last:
            ctx = ctx + g1c * yc
            ctx = ctx + g2c * peer_ffn(modulate(rmsnorm(ctx, norm2_g[layer]), sh2c, sc2c),
                                       peer_wq[layer], peer_keys[layer], peer_u[layer], peer_v[layer])
    return rmsnorm(x, final_norm_g)


_drawn_inputs = setup_inputs


def setup_inputs(seed=0):
    import zlib

    import numpy as np

    out = dict(_drawn_inputs(seed))
    spreads = {}
    factors = {'q_norm_g': 6.876, 'k_norm_g': 7.497, 'rg_ba': 22.593, 'rg_bx': 6.772}
    for name, (base, spread) in spreads.items():
        noise = np.random.default_rng([zlib.crc32(name.encode()), seed]).standard_normal(out[name].shape)
        drawn = base * np.exp(spread * noise) if base else spread * noise
        out[name] = jnp.asarray(drawn.astype(out[name].dtype))
    for name, factor in factors.items():
        out[name] = (out[name] * factor).astype(out[name].dtype)
    return out
```

```python
from contextlib import ExitStack

import numpy as np

import concourse.bass as bass
from concourse import mybir

ALU = mybir.AluOpType
ACT = mybir.ActivationFunctionType
AX = mybir.AxisListType.X
F32 = mybir.dt.float32
U32 = mybir.dt.uint32

P = 128
D = 1024
DC = D // P
SEQ, CTX = 512, 256
CT, LT = CTX // P, SEQ // P
NT = CT + LT
TOK = NT * P
EPS = 1e-6
GRID_W = 64
HD = 128
NQ, NKV = 4, 2
NQK = NQ + NKV
GROUPS = 4
AW = GROUPS * P
DR = 1280
RB = DR // P
CONV = 4
HEADS = 8
KEYS = 128
TOPK = 16
SLOTS = HEADS * TOPK
BIG = -3.0e38
RAW_CTX, RAW_LAT = 2, 2 + CTX + 1 + 2
OUT_CTX, OUT_LAT = RAW_CTX - 2, RAW_LAT - 2
XCW = OUT_LAT + SEQ + 1
HALF = XCW // 2
RAWW = XCW + CONV - 1


def stream(t):
    return (t + LT - CT) // LT


class Steps:

    def __init__(self, eng, sem):
        self.eng, self.sem, self.n = eng, sem, 0

    def did(self, ins):
        ins.then_inc(self.sem, 1)
        self.n += 1
        return self.n

    def settle(self):
        self.eng.wait_ge(self.sem, self.n)

    def then(self, ins):
        self.did(ins)
        self.settle()

    def restart(self):
        self.settle()
        self.eng.sem_clear(self.sem)
        self.n = 0


class Pool:

    def __init__(self, nc, ctx, stage):
        self.nc, self.ctx, self.stage = nc, ctx, stage
        self.sems = []
        ctx.callback(self.clear)

    def sb(self, name, shape, dt=F32):
        return self.ctx.enter_context(self.nc.sbuf_tensor(f"{self.stage}_{name}", shape, dt))

    def ps(self, name, shape):
        return self.ctx.enter_context(self.nc.psum_tensor(f"{self.stage}_{name}", shape, F32))

    def sem(self, name):
        self.sems.append(self.nc.alloc_semaphore(f"{self.stage}_{name}"))
        return self.sems[-1]

    def clear(self):
        if self.sems:
            with self.nc.Block() as block:

                @block.gpsimd
                def _(pool):
                    self.nc.clear_and_free_semaphores(self.sems)




def modulation_stage(nc, io, mod_dram):
    NCH = 2 * 6 * D // 512
    RING = 4
    with ExitStack() as ctx:
        m = Pool(nc, ctx, "mod")
        cv = m.sb("cv", [P, 2, DC])
        sg = m.sb("sg", [P, 2, DC])
        sT = m.sb("sT", [P, 2, DC])
        W = m.sb("W", [P, RING, DC, 512])
        bias = m.sb("bias", [2, 12 * D])
        rows = m.sb("rows", [2, 12 * D])
        acc = m.ps("acc", [P, RING, 512])
        c_in, bias_in = m.sem("c_in"), m.sem("bias_in")
        w_in = [m.sem(f"w_in{r}") for r in range(RING)]
        chunk_done, sig_ready, s_ready = m.sem("chunk_done"), m.sem("sig_ready"), m.sem("s_ready")
        acc_free, stored = m.sem("acc_free"), m.sem("stored")

        with nc.Block() as block:

            @block.sync
            def _(sp):
                sp.dma_start(cv[:, 0, :], io["c_ctx"].rearrange("(p k) -> p k", k=DC)).then_inc(c_in, 16)
                sp.dma_start(cv[:, 1, :], io["c"].rearrange("a (p k) -> p (a k)", k=DC)).then_inc(c_in, 16)
                sp.dma_start(bias[:], io["mod_b"].rearrange("l n -> (l n)").partition_broadcast(2)).then_inc(
                    bias_in, 16
                )
                for layer in range(2):
                    w = io["mod_w"][layer].rearrange("(p k) n -> p k n", k=DC)
                    with sp.Fori(0, NCH // 2 // RING) as i:
                        for r in range(RING):
                            sp.wait_ge(chunk_done, i * RING + (layer * NCH // 2 + r + 1))
                            sp.dma_start(W[:, r, :, :], w[:, :, bass.ds((i * RING + r) * 512, 512)]).then_inc(
                                w_in[r], 16
                            )
                sp.wait_ge(acc_free, RING + NCH)
                sp.dma_start(mod_dram.rearrange("s l j d -> s (l j d)"), rows[:]).then_inc(stored, 16)
                sp.wait_ge(stored, 16)

            @block.scalar
            def _(act):
                act.wait_ge(c_in, 32)
                nc.scalar.activation(sg[:], cv[:], ACT.Sigmoid).then_inc(sig_ready, 1)

            @block.vector
            def _(dve):
                dve.sem_inc(acc_free, RING)
                dve.wait_ge(sig_ready, 1)
                nc.vector.tensor_tensor(sT[:], sg[:], cv[:], ALU.mult).then_inc(s_ready, 1)
                dve.wait_ge(bias_in, 16)
                with dve.Fori(0, NCH // RING) as i:
                    for r in range(RING):
                        dve.wait_ge(chunk_done, i * RING + (RING + r + 1))
                        cols = bass.ds((i * RING + r) * 512, 512)
                        nc.vector.tensor_tensor(rows[:, cols], acc[0:2, r, :], bias[:, cols], ALU.add).then_inc(
                            acc_free, 1
                        )

            @block.tensor
            def _(pe):
                pe.sem_inc(chunk_done, RING)
                pe.wait_ge(s_ready, 1)
                with pe.Fori(0, NCH // RING) as i:
                    for r in range(RING):
                        pe.wait_ge(w_in[r], i * 16 + 16)
                        pe.wait_ge(acc_free, i * RING + (r + 1))
                        for k in range(DC):
                            ins = nc.tensor.matmul(
                                acc[0:2, r, :], sT[:, :, k], W[:, r, k, :], start=(k == 0), stop=(k == DC - 1)
                            )
                        ins.then_inc(chunk_done, 1)




class NormTranspose:

    def __init__(self, m, X, ident, junk, normbc, hT, hN, TR):
        self.X, self.ident, self.junk, self.hT, self.hN, self.TR = X, ident, junk, hT, hN, TR
        self.A = normbc[:, 0 : 2 * D].rearrange("p (s d) -> p s d", s=2)
        self.B = normbc[:, 2 * D : 4 * D].rearrange("p (s d) -> p s d", s=2)
        self.gain = normbc[:, 4 * D : 5 * D]
        self.ss = m.sb("ss", [P, NT])
        self.std = m.sb("std", [P, NT])
        self.rstd = m.sb("rstd", [P, NT])
        self.mod_in, self.sq_done, self.std_ready = m.sem("mod_in"), m.sem("sq_done"), m.sem("std_ready")
        self.h_ready, self.tr_ready, self.hT_ready = m.sem("h_ready"), m.sem("tr_ready"), m.sem("hT_ready")

    def load(self, nc, sp, io, mod_dram, layer):
        for s in range(2):
            sp.dma_start(self.A[:, s, :], mod_dram[s, layer, 1].partition_broadcast(P)).then_inc(self.mod_in, 16)
            sp.dma_start(self.B[:, s, :], mod_dram[s, layer, 0].partition_broadcast(P)).then_inc(self.mod_in, 16)
        sp.dma_start(self.gain, io["norm1_g"][layer].partition_broadcast(P)).then_inc(self.mod_in, 16)

    def scalar_sums(self, nc, act, x_wait):
        for t in range(NT):
            x_wait(act, t)
            if t:
                act.wait_ge(self.sq_done, t)
            nc.scalar.activation(
                self.junk, self.X[:, t, :], ACT.Square, accum_out=self.ss[:, t : t + 1]
            ).then_inc(self.sq_done, 1)
        act.wait_ge(self.sq_done, NT)
        nc.scalar.activation(self.std[:], self.ss[:], ACT.Sqrt, bias=self.eps[:, 0:1], scale=1.0 / D).then_inc(self.std_ready, 1)

    def scalar_out(self, nc, act):
        for t in range(NT):
            act.wait_ge(self.tr_ready, t + 1)
            for h in range(2):
                nc.scalar.copy(
                    self.hT[:, 4 * h : 4 * h + 4, t * P : (t + 1) * P],
                    self.TR[:, t % 2, 512 * h : 512 * h + 512].rearrange("p (c q) -> p c q", c=4),
                ).then_inc(self.hT_ready, 1)

    def vector(self, nc, dve, st):
        dve.wait_ge(self.mod_in, 16 * 5)
        for s in range(2):
            st.did(
                nc.vector.scalar_tensor_tensor(
                    out=self.A[:, s, :], in0=self.A[:, s, :], scalar=1.0, in1=self.gain, op0=ALU.add, op1=ALU.mult
                )
            )
        dve.wait_ge(self.std_ready, 1)
        st.then(nc.vector.reciprocal(self.rstd[:], self.std[:]))
        for t in range(NT):
            s = stream(t)
            h = self.hN[:, t % 2, :]
            if t >= 2:
                dve.wait_ge(self.tr_ready, t - 1)
            st.then(
                nc.vector.scalar_tensor_tensor(
                    out=h, in0=self.X[:, t, :], scalar=self.rstd[:, t : t + 1], in1=self.A[:, s, :],
                    op0=ALU.mult, op1=ALU.mult,
                )
            )
            nc.vector.tensor_tensor(h, h, self.B[:, s, :], ALU.add).then_inc(self.h_ready, 1)

    def tensor(self, nc, pe):
        for t in range(NT):
            pe.wait_ge(self.h_ready, t + 1)
            if t >= 2:
                pe.wait_ge(self.hT_ready, 2 * (t - 1))
            for c in range(DC):
                ins = nc.tensor.transpose(
                    self.TR[:, t % 2, c * P : (c + 1) * P], self.hN[:, t % 2, c * P : (c + 1) * P], self.ident[:]
                )
            ins.then_inc(self.tr_ready, 1)




def mixer_ab_stage(nc, io, mod_dram, X, ident, ones, eps):
    SC = float(HD) ** -0.5
    HT = TOK // 2
    with ExitStack() as ctx:
        m = Pool(nc, ctx, "ab")
        normbc = m.sb("normbc", [P, 5 * D])
        qk = normbc[:, 0 : NQK * TOK].rearrange("p (j t) -> p j t", j=NQK)
        hN = m.sb("hN", [P, 2, D])
        hT = m.sb("hT", [P, DC, TOK])
        yA = hT[:, 0:NQ, :]
        attn = hT[:, NQ:DC, :]
        prob = [attn[:, i, :] for i in range(2)]
        probT = [attn[:, 2 + i, :].rearrange("p (k q) -> p k q", q=P) for i in range(2)]
        WA = m.sb("WA", [P, DC, D])
        WB = m.sb("WB", [P, DC, D])
        uT = m.sb("uT", [P, GROUPS, TOK])
        vv = m.sb("vv", [P, NT, AW])
        vS = m.sb("vS", [P, NT, NKV * HD])
        g1 = m.sb("g1", [P, 2, D])
        sq = m.sb("sq", [P, 2, HT])
        qraw = m.sb("qraw", [P, 2, HT])
        stdq = m.sb("stdq", [P, 2, HT])
        qn = m.sb("qn", [P, 2, HT])
        t12 = m.sb("t12", [P, 2, HT])
        tmp = t12[:, :, :].rearrange("p a b -> p (a b)")[:, 0:512]
        cos, sin = m.sb("cos", [P, TOK]), m.sb("sin", [P, TOK])
        rotm = m.sb("rotm", [P, P])
        wsT = m.sb("wsT", [P, GROUPS, P])
        bsb = m.sb("bsb", [P, GROUPS, P])
        gcol = m.sb("gcol", [P, GROUPS])
        qkg = m.sb("qkg", [P, 2])
        ssv, stdv, rv = m.sb("ssv", [P, NT * GROUPS]), m.sb("stdv", [P, NT * GROUPS]), m.sb("rv", [P, NT * GROUPS])
        mx, nm = m.sb("mx", [P, 2]), m.sb("nm", [P, 2])
        psum_p, rp = m.sb("psum_p", [P, 2]), m.sb("rp", [P, 2])
        TR = m.ps("TR", [P, 2, D])
        MM = m.ps("MM", [P, 4, 512])

        norm = NormTranspose(m, X, ident, uT[:, 0:2, :].rearrange("p a b -> p (a b)")[:, 0:D], normbc, hT, hN, TR)
        norm.eps = eps
        x_in = [m.sem(f"x_in{t}") for t in range(NT)]
        wa_in, wb_in, wout_in, const_in, g1_in = (m.sem(x) for x in ("wa_in", "wb_in", "wout_in", "const_in", "g1_in"))
        mm_ready, mm_free = m.sem("mm_ready"), m.sem("mm_free")
        ssq_ready, stdq_ready, qn_ready, rot_ready, qk_done = (
            m.sem(x) for x in ("ssq_ready", "stdq_ready", "qn_ready", "rot_ready", "qk_done")
        )
        ssv_ready, stdv_ready, vvn_ready, gate_ready, gm_done = (
            m.sem(x) for x in ("ssv_ready", "stdv_ready", "vvn_ready", "gate_ready", "gm_done")
        )
        sc_ready, nm_ready, p_ready, pn_ready, ptr_ready, pt_ready, o_ready, o_done = (
            m.sem(x)
            for x in ("sc_ready", "nm_ready", "p_ready", "pn_ready", "ptr_ready", "pt_ready", "o_ready", "o_done")
        )
        y_ready, y_done, dve_step, act_step = m.sem("y_ready"), m.sem("y_done"), m.sem("dve_step"), m.sem("act_step")

        U0, V0, S0, Q0 = 0, 8, 8 + NT, 8 + 2 * NT
        QU = NQK * 2
        units = [(t, j) for t in range(NT) for j in range(NQ)]

        def nkeys(t):
            return CTX if t < CT else TOK

        with nc.Block() as block:

            @block.sync
            def _(sp):
                norm.load(nc, sp, io, mod_dram, 0)
                for t in range(NT):
                    src = io["ctx"][0, t * P : (t + 1) * P, :] if t < CT else io["x"][0, (t - CT) * P : (t - CT + 1) * P, :]
                    sp.dma_start(X[:, t, :], src).then_inc(x_in[t], 16)
                w = io["ab_w_in"][0].rearrange("(c p) n -> p c n", p=P)
                sp.dma_start(WA[:], w[:, :, 0:D]).then_inc(wa_in, 16)
                sp.dma_start(WB[:], w[:, :, D : 2 * D]).then_inc(wb_in, 16)
                bs_row = io["gmlp_bs"].rearrange("o g q -> (o g q)")
                for dst, src in (
                    (cos[:], io["cos"]), (sin[:], io["sin"]), (rotm[:], io["rotm"]), (wsT[:], io["wsT"]),
                    (bsb[:].rearrange("p g q -> p (g q)"), bs_row.partition_broadcast(P)),
                    (gcol[:], io["gmlp_gT"]), (qkg[:], io["qk_gT"]),
                ):
                    sp.dma_start(dst, src).then_inc(const_in, 16)
                for s in range(2):
                    sp.dma_start(g1[:, s, :], mod_dram[s, 0, 2].partition_broadcast(P)).then_inc(g1_in, 16)
                sp.wait_ge(mm_ready, S0)
                sp.dma_start(WA[:], io["ab_w_out"][0].rearrange("(c p) n -> p c n", p=P)).then_inc(wout_in, 16)

            @block.scalar
            def _(act):
                st = Steps(act, act_step)
                norm.scalar_sums(nc, act, lambda e, t: e.wait_ge(x_in[t], 16))
                norm.scalar_out(nc, act)
                for g in range(GROUPS):
                    for h in range(2):
                        n = U0 + 2 * g + h
                        act.wait_ge(mm_ready, n + 1)
                        nc.scalar.activation(
                            uT[:, g, h * HT : (h + 1) * HT], MM[:, n % 4, 0:HT], ACT.Gelu_apprx_tanh
                        ).then_inc(mm_free, 1)
                for t in range(NT):
                    n = V0 + t
                    act.wait_ge(mm_ready, n + 1)
                    nc.scalar.activation(vv[:, t, :], MM[:, n % 4, :], ACT.Gelu_apprx_tanh).then_inc(mm_free, 1)
                for t in range(NT):
                    n = S0 + t
                    act.wait_ge(mm_ready, n + 1)
                    nc.scalar.copy(vS[:, t, :], MM[:, n % 4, 0 : NKV * HD]).then_inc(mm_free, 1)
                act.wait_ge(ssv_ready, 1)
                nc.scalar.activation(stdv[:], ssv[:], ACT.Sqrt, bias=eps[:, 0:1], scale=1.0 / P).then_inc(stdv_ready, 1)
                act.wait_ge(const_in, 16 * 7)
                for u in range(QU + 1):
                    if u < QU:
                        n, par = Q0 + u, u % 2
                        act.wait_ge(mm_ready, n + 1)
                        if u >= 2:
                            act.wait_ge(ssq_ready, u - 1)
                            act.wait_ge(qn_ready, u - 1)
                        st.did(nc.scalar.square(sq[:, par, :], MM[:, n % 4, 0:HT]))
                        kind = 0 if u // 2 < NQ else 1
                        st.settle()
                        nc.scalar.activation(
                            qraw[:, par, :], MM[:, n % 4, 0:HT], ACT.Copy, scale=qkg[:, kind : kind + 1]
                        ).then_inc(mm_free, 1)
                    if u >= 1:
                        v, par = u - 1, (u - 1) % 2
                        act.wait_ge(ssq_ready, v + 1)
                        if v >= 2:
                            act.wait_ge(qn_ready, v - 1)
                        nc.scalar.activation(
                            stdq[:, par, :], TR[:, par, 0:HT], ACT.Sqrt, bias=eps[:, 0:1], scale=1.0 / HD
                        ).then_inc(stdq_ready, 1)
                for u in range(len(units) + 1):
                    if u < len(units):
                        t, j = units[u]
                        nk, par = nkeys(t), u % 2
                        act.wait_ge(nm_ready, u + 1)
                        if u >= 2:
                            act.wait_ge(ptr_ready, u - 1)
                        w = min(nk, HT)
                        nc.scalar.activation(
                            prob[par][:, 0:nk].rearrange("p (a k) -> p a k", k=w),
                            TR[:, par, :].rearrange("p (a k) -> p a k", a=2)[:, 0 : nk // w, 0:w],
                            ACT.Exp, bias=nm[:, par : par + 1], scale=SC, accum_out=psum_p[:, par : par + 1],
                        ).then_inc(p_ready, 1)
                    if u >= 1:
                        v = u - 1
                        nk, par = nkeys(units[v][0]), v % 2
                        act.wait_ge(ptr_ready, v + 1)
                        if v >= 2:
                            act.wait_ge(o_ready, v - 1)
                        k3 = min(nk // P, 3)
                        nc.scalar.copy(
                            probT[par][:, 0 : nk // P, :].rearrange("p (a k) q -> p a k q", k=k3),
                            MM[:, 0 : nk // P // k3, 0 : k3 * P].rearrange("p a (k q) -> p a k q", q=P),
                        ).then_inc(pt_ready, 1)

            @block.vector
            def _(dve):
                st = Steps(dve, dve_step)
                norm.vector(nc, dve, st)
                for t in range(NT):
                    dve.wait_ge(mm_free, V0 + t + 1)
                    st.then(nc.vector.tensor_tensor(tmp, vv[:, t, :], vv[:, t, :], ALU.mult))
                    ins = nc.vector.reduce_sum(
                        ssv[:, GROUPS * t : GROUPS * (t + 1)], tmp.rearrange("p (g c) -> p g c", g=GROUPS), AX
                    )
                    st.then(ins)
                dve.sem_inc(ssv_ready, 1)
                dve.wait_ge(stdv_ready, 1)
                st.then(nc.vector.reciprocal(rv[:], stdv[:]))
                for t in range(NT):
                    v3 = vv[:, t, :].rearrange("p (g c) -> p g c", g=GROUPS)
                    nc.vector.tensor_tensor(
                        v3, v3, rv[:, GROUPS * t : GROUPS * (t + 1)].unsqueeze(2).to_broadcast([P, GROUPS, P]), ALU.mult
                    ).then_inc(vvn_ready, 1)
                dve.wait_ge(const_in, 16 * 7)
                for u in range(QU + 1):
                    if u < QU:
                        par = u % 2
                        dve.wait_ge(stdq_ready, u + 1)
                        st.then(nc.vector.reciprocal(stdq[:, par, :], stdq[:, par, :]))
                        dve.wait_ge(mm_free, Q0 + u + 1)
                        nc.vector.tensor_tensor(qn[:, par, :], qraw[:, par, :], stdq[:, par, :], ALU.mult).then_inc(
                            qn_ready, 1
                        )
                    if u >= 1:
                        v, par = u - 1, (u - 1) % 2
                        j, h = v // 2, v % 2
                        cols = slice(h * HT, (h + 1) * HT)
                        dve.wait_ge(rot_ready, v + 1)
                        dve.wait_ge(qn_ready, v + 1)
                        st.did(nc.vector.tensor_tensor(t12[:, 0, :], qn[:, par, :], cos[:, cols], ALU.mult))
                        st.then(nc.vector.tensor_tensor(t12[:, 1, :], TR[:, par, 512 : 512 + HT], sin[:, cols], ALU.mult))
                        nc.vector.tensor_tensor(qk[:, j, cols], t12[:, 0, :], t12[:, 1, :], ALU.add).then_inc(qk_done, 1)
                        dve.wait_ge(qk_done, v + 1)
                for t in range(NT):
                    dve.wait_ge(gate_ready, t + 1)
                    for g in range(GROUPS):
                        st.did(
                            nc.vector.scalar_tensor_tensor(
                                out=tmp[:, g * P : (g + 1) * P], in0=MM[:, t % 4, g * P : (g + 1) * P],
                                scalar=gcol[:, g : g + 1], in1=bsb[:, g, :], op0=ALU.mult, op1=ALU.add,
                            )
                        )
                    st.settle()
                    ut = uT[:, :, t * P : (t + 1) * P]
                    nc.vector.tensor_tensor(ut, ut, tmp.rearrange("p (g q) -> p g q", g=GROUPS), ALU.mult).then_inc(
                        gm_done, 1
                    )
                    dve.wait_ge(gm_done, t + 1)
                for u in range(len(units) + 2):
                    if u < len(units):
                        t, j = units[u]
                        nk, par = nkeys(t), u % 2
                        w = min(nk, HT)
                        dve.wait_ge(sc_ready, u + 1)
                        if u >= 2:
                            dve.wait_ge(p_ready, u - 1)
                        st.then(
                            nc.vector.tensor_reduce(
                                mx[:, par : par + 1],
                                TR[:, par, :].rearrange("p (a k) -> p a k", a=2)[:, 0 : nk // w, 0:w],
                                mybir.AxisListType.XY, ALU.max,
                            )
                        )
                        nc.vector.tensor_scalar(nm[:, par : par + 1], mx[:, par : par + 1], -SC, None, ALU.mult).then_inc(
                            nm_ready, 1
                        )
                    if 1 <= u <= len(units):
                        v, par = u - 1, (u - 1) % 2
                        nk = nkeys(units[v][0])
                        dve.wait_ge(p_ready, v + 1)
                        st.then(nc.vector.reciprocal(rp[:, par : par + 1], psum_p[:, par : par + 1]))
                        nc.vector.tensor_scalar(
                            prob[par][:, 0:nk], prob[par][:, 0:nk], rp[:, par : par + 1], None, ALU.mult
                        ).then_inc(pn_ready, 1)
                    if u >= 2:
                        v, par = u - 2, u % 2
                        t, j = units[v]
                        dve.wait_ge(o_ready, v + 1)
                        nc.vector.tensor_copy(yA[:, j, t * P : (t + 1) * P], MM[:, 2 + par, 0:P]).then_inc(o_done, 1)
                dve.wait_ge(g1_in, 32)
                for n in range(2 * NT):
                    t, h = n // 2, n % 2
                    cols = slice(512 * h, 512 * h + 512)
                    dve.wait_ge(y_ready, n + 1)
                    if n:
                        dve.wait_ge(y_done, n)
                    st.then(
                        nc.vector.tensor_tensor(
                            tmp, TR[:, n % 4 // 2, 512 * (n % 2) : 512 * (n % 2) + 512], g1[:, stream(t), cols], ALU.mult
                        )
                    )
                    nc.vector.tensor_tensor(X[:, t, cols], X[:, t, cols], tmp, ALU.add).then_inc(y_done, 1)

            @block.tensor
            def _(pe):
                norm.tensor(nc, pe)
                pe.wait_ge(norm.hT_ready, 2 * NT)

                def bank(n):
                    if n >= 4:
                        pe.wait_ge(mm_free, n - 3)
                    return MM[:, n % 4, :]

                def project_cols(n, W, c0, h):
                    out = bank(n)[:, 0:HT]
                    for c in range(DC):
                        ins = nc.tensor.matmul(
                            out, W[:, c, c0 : c0 + P], hT[:, c, h * HT : (h + 1) * HT], start=(c == 0), stop=(c == DC - 1)
                        )
                    ins.then_inc(mm_ready, 1)

                def project_rows(n, W, c0, width, t):
                    out = bank(n)[:, 0:width]
                    for c in range(DC):
                        ins = nc.tensor.matmul(
                            out, hT[:, c, t * P : (t + 1) * P], W[:, c, c0 : c0 + width], start=(c == 0), stop=(c == DC - 1)
                        )
                    ins.then_inc(mm_ready, 1)

                pe.wait_ge(wa_in, 16)
                for g in range(GROUPS):
                    for h in range(2):
                        project_cols(U0 + 2 * g + h, WA, g * P, h)
                for t in range(NT):
                    project_rows(V0 + t, WA, AW, AW, t)
                pe.wait_ge(wb_in, 16)
                for t in range(NT):
                    project_rows(S0 + t, WB, NQK * HD, NKV * HD, t)
                pe.wait_ge(const_in, 16 * 7)
                for u in range(QU + 2):
                    if u < QU:
                        project_cols(Q0 + u, WB, (u // 2) * HD, u % 2)
                    if 1 <= u <= QU:
                        v, par = u - 1, (u - 1) % 2
                        pe.wait_ge(mm_free, Q0 + v + 1)
                        if v >= 2:
                            pe.wait_ge(stdq_ready, v - 1)
                        nc.tensor.matmul(TR[:, par, 0:HT], ones[:], sq[:, par, :], start=True, stop=True).then_inc(
                            ssq_ready, 1
                        )
                    if u >= 2:
                        v, par = u - 2, u % 2
                        pe.wait_ge(qn_ready, v + 1)
                        if v >= 2:
                            pe.wait_ge(qk_done, v - 1)
                        nc.tensor.matmul(
                            TR[:, par, 512 : 512 + HT], rotm[:], qn[:, par, :], start=True, stop=True
                        ).then_inc(rot_ready, 1)
                pe.wait_ge(mm_free, Q0 + QU)
                for t in range(NT):
                    pe.wait_ge(vvn_ready, t + 1)
                    if t >= 4:
                        pe.wait_ge(gm_done, t - 3)
                    for g in range(GROUPS):
                        ins = nc.tensor.matmul(
                            MM[:, t % 4, g * P : (g + 1) * P], vv[:, t, g * P : (g + 1) * P], wsT[:, g, :],
                            start=True, stop=True,
                        )
                    ins.then_inc(gate_ready, 1)

                def scores(u):
                    t, j = units[u]
                    nk, par = nkeys(t), u % 2
                    w = min(nk, HT)
                    if u >= 2:
                        pe.wait_ge(p_ready, u - 1)
                    for a in range(nk // w):
                        ins = nc.tensor.matmul(
                            TR[:, par, 512 * a : 512 * a + w], qk[:, j, t * P : (t + 1) * P],
                            qk[:, NQ + j // (NQ // NKV), a * w : (a + 1) * w], start=True, stop=True,
                        )
                    ins.then_inc(sc_ready, 1)

                def turn(u):
                    nk, par = nkeys(units[u][0]), u % 2
                    pe.wait_ge(pn_ready, u + 1)
                    if u >= 1:
                        pe.wait_ge(pt_ready, u)
                    k3 = min(nk // P, 3)
                    for k in range(nk // P):
                        ins = nc.tensor.transpose(
                            MM[:, k // k3, (k % k3) * P : (k % k3 + 1) * P], prob[par][:, k * P : (k + 1) * P], ident[:]
                        )
                    ins.then_inc(ptr_ready, 1)

                def weigh(u):
                    t, j = units[u]
                    nk, par = nkeys(t), u % 2
                    kv = j // (NQ // NKV)
                    pe.wait_ge(pt_ready, u + 1)
                    if u >= 2:
                        pe.wait_ge(o_done, u - 1)
                    for k in range(nk // P):
                        ins = nc.tensor.matmul(
                            MM[:, 2 + par, 0:P], vS[:, k, kv * HD : (kv + 1) * HD], probT[par][:, k, :],
                            start=(k == 0), stop=(k == nk // P - 1),
                        )
                    ins.then_inc(o_ready, 1)

                pe.wait_ge(qk_done, QU)
                pe.wait_ge(gm_done, NT)
                for u in range(-1, len(units) + 1):
                    if u + 1 < len(units):
                        scores(u + 1)
                    if 0 <= u < len(units):
                        turn(u)
                    if u >= 1:
                        weigh(u - 1)
                pe.wait_ge(o_done, len(units))
                pe.wait_ge(wout_in, 16)
                pe.wait_ge(p_ready, len(units))
                for n in range(2 * NT):
                    t, h = n // 2, n % 2
                    if n >= 4:
                        pe.wait_ge(y_done, n - 3)
                    out = TR[:, n % 4 // 2, 512 * (n % 2) : 512 * (n % 2) + 512]
                    for k in range(DC):
                        src = uT[:, k, :] if k < GROUPS else yA[:, k - GROUPS, :]
                        ins = nc.tensor.matmul(
                            out, src[:, t * P : (t + 1) * P], WA[:, k, 512 * h : 512 * h + 512],
                            start=(k == 0), stop=(k == DC - 1),
                        )
                    ins.then_inc(y_ready, 1)




def peer_stage(nc, io, mod_dram, X, ident, eps, layer, T0, out):
    M = NT - T0
    RING = 4
    u_tab, v_tab = io[f"peer_u{layer}"], io[f"peer_v{layer}"]
    with ExitStack() as ctx:
        m = Pool(nc, ctx, f"peer{layer}")
        wq = m.sb("wq", [P, DC, 2 * HEADS * KEYS])
        keys = m.sb("keys", [P, 2 * HEADS, KEYS])
        A, B, g2 = m.sb("A", [P, 2, D]), m.sb("B", [P, 2, D]), m.sb("g2", [P, 2, D])
        gain = m.sb("gain", [P, D])
        iota = m.sb("iota", [P, TOPK])
        U, V = m.sb("U", [P, RING, D]), m.sb("V", [P, RING, D])
        h_next, h_cur = m.sb("h_next", [P, D]), m.sb("h_cur", [P, D])
        hT = m.sb("hT", [P, DC, P])
        qT = m.sb("qT", [P, 2, 2, P])
        diag = m.sb("diag", [P, RING, P])
        h_tmp = m.sb("h_tmp", [P, D])
        ss, rstd = m.sb("ss", [P, M]), m.sb("rstd", [P, M])
        S, S2 = m.sb("S", [P, 2, KEYS]), m.sb("S2", [P, 2, KEYS])
        best, ibest = m.sb("best", [P, 2, TOPK]), m.sb("ibest", [P, 2, TOPK], U32)
        cand, cand2 = m.sb("cand", [P, TOPK, TOPK]), m.sb("cand2", [P, TOPK, TOPK])
        top, pos = m.sb("top", [P, TOPK]), m.sb("pos", [P, TOPK], U32)
        half_pos = m.sb("half_pos", [P, 2, TOPK], U32)
        hot = m.sb("hot", [P, 2, TOPK, TOPK])
        half_idx = m.sb("half_idx", [P, 2, TOPK])
        experts = m.sb("experts", [P, SLOTS], U32)
        zero = m.sb("zero", [P, 1], U32)
        scores = m.sb("scores", [P, M * SLOTS])
        gate = m.sb("gate", [P, HEADS, TOPK])
        gsum = m.sb("gsum", [P, HEADS])
        idx = m.sb("idx", [P, 2, TOPK], U32)
        dots, act_out, wgt = m.sb("dots", [P, 2, TOPK]), m.sb("act_out", [P, 2, TOPK]), m.sb("wgt", [P, 2, TOPK])
        psT = m.ps("psT", [P, D])
        psq = m.ps("psq", [P, 2, 512])
        psS = m.ps("psS", [P, 2, 512])
        psY = m.ps("psY", [P, D])

        const_in = m.sem("const_in")
        wq_in = m.sem("wq_in")
        sq_done, std_ready, h_ready, tr_ready, hT_ready = (
            m.sem(x) for x in ("sq_done", "std_ready", "h_ready", "tr_ready", "hT_ready")
        )
        q_ready, q_copied, s_ready, chosen = (m.sem(x) for x in ("q_ready", "q_copied", "s_ready", "chosen"))
        g_shifted, g_exp = m.sem("g_shifted"), m.sem("g_exp")
        u_in = [m.sem(f"u_in{r}") for r in range(RING)]
        v_in = [m.sem(f"v_in{r}") for r in range(RING)]
        u_used, v_used = m.sem("u_used"), m.sem("v_used")
        act_ready, w_ready, diag_ready, y_ready, y_taken, idx_copied, dve_step, x_done = (
            m.sem(x)
            for x in ("act_ready", "w_ready", "diag_ready", "y_ready", "y_taken", "idx_copied", "dve_step", "x_done")
        )
        zero_set = m.sem("zero_set")
        gain_free, gain_in = m.sem("gain_free"), m.sem("gain_in")
        fin_sq, fin_std, fin_done, stored = (m.sem(x) for x in ("fin_sq", "fin_std", "fin_done", "stored"))

        def turns(eng, turn):
            turn(-1, choose=True, combine=False)
            turn(0, choose=True, combine=True)
            with eng.Fori(1, M - 1) as j:
                turn(j, choose=True, combine=True)
            turn(M - 1, choose=False, combine=True)

        def first(j, n=0):
            return isinstance(j, int) and j <= n

        with nc.Block() as block:

            @block.sync
            def _(sp):
                for s in range(2):
                    for dst, k in ((A, 4), (B, 3), (g2, 5)):
                        sp.dma_start(dst[:, s, :], mod_dram[s, layer, k].partition_broadcast(P)).then_inc(const_in, 16)
                sp.dma_start(gain[:], io["norm2_g"][layer].partition_broadcast(P)).then_inc(const_in, 16)
                sp.dma_start(keys[:], io["keysT"][layer]).then_inc(const_in, 16)
                sp.dma_start(iota[:], io["iota"]).then_inc(const_in, 16)
                w = io["peer_wq"][layer].rearrange("(c p) n -> p c n", p=P)
                sp.dma_start(wq[:], w).then_inc(wq_in, 16)
                if out is not None:
                    o = out.rearrange("o (t p) d -> p (o t) d", p=P)
                    sp.wait_ge(gain_free, 1)
                    sp.dma_start(gain[:], io["final_norm_g"].partition_broadcast(P)).then_inc(gain_in, 16)
                    sp.wait_ge(fin_done, M)
                    sp.dma_start(o, X[:, T0:NT, :]).then_inc(stored, 16)
                    sp.wait_ge(stored, 16)

            @block.gpsimd
            def _(pool):
                def take(n_par, hd, k):
                    src = experts[:, hd * TOPK + k : hd * TOPK + k + 1]
                    pool.tensor_tensor(idx[:, n_par, k : k + 1], src, zero[:], ALU.add).then_inc(idx_copied, 1)

                def rows(table, ring, n_par, k, arrived):
                    pool.indirect_dma_start(
                        ring[:, k % RING, :], None, table, bass.IndirectOffsetOnAxis(ap=idx[:, n_par, k : k + 1], axis=0)
                    ).then_inc(arrived[k % RING], 16)

                pool.memset(zero[:], 0).then_inc(zero_set, 1)
                pool.wait_ge(zero_set, 1)
                pool.wait_ge(chosen, 1)
                for k in range(TOPK):
                    take(0, 0, k)
                for k in range(TOPK):
                    pool.wait_ge(idx_copied, k + 1)
                    pool.wait_ge(u_used, k + 1)
                    rows(u_tab, U, 0, k, u_in)
                pool.wait_ge(chosen, 2)
                take(1, 1, 0)

                def head(j, hd, heads_left):
                    n, par = j * HEADS + hd, hd % 2
                    for k in range(TOPK):
                        pool.wait_ge(v_used, n * TOPK + (k + 1))
                        if heads_left >= 1:
                            pool.wait_ge(u_used, n * TOPK + (TOPK + k + 1))
                            pool.wait_ge(idx_copied, n * TOPK + (TOPK + k + 1))
                            if k < TOPK - 1:
                                take(1 - par, (hd + 1) % HEADS, k + 1)
                            elif heads_left >= 2:
                                pool.wait_ge(chosen, n + 3)
                                take(par, (hd + 2) % HEADS, 0)
                        rows(v_tab, V, par, k, v_in)
                        if heads_left >= 1:
                            rows(u_tab, U, 1 - par, k, u_in)

                for hd in range(HEADS):
                    head(0, hd, HEADS)
                with pool.Fori(1, M - 1) as j:
                    for hd in range(HEADS):
                        head(j, hd, HEADS)
                for hd in range(HEADS):
                    head(M - 1, hd, HEADS - 1 - hd)

            @block.scalar
            def _(act):
                for t in range(M):
                    nc.scalar.activation(
                        V[:, t % RING, :], X[:, T0 + t, :], ACT.Square, accum_out=ss[:, t : t + 1]
                    ).then_inc(sq_done, 1)
                    if t < M - 1 and t % RING == RING - 1:
                        act.wait_ge(sq_done, t + 1)
                act.wait_ge(sq_done, M)
                nc.scalar.activation(rstd[:], ss[:], ACT.Sqrt, bias=eps[:, 0:1], scale=1.0 / D).then_inc(std_ready, 1)

                def turn(j, choose, combine):
                    c = j + 1
                    if choose:
                        act.wait_ge(tr_ready, c + 1)
                        for h in range(2):
                            nc.scalar.copy(
                                hT[:, 4 * h : 4 * h + 4, :],
                                psT[:, 512 * h : 512 * h + 512].rearrange("p (c q) -> p c q", c=4),
                            ).then_inc(hT_ready, 1)
                    if combine:
                        act.wait_ge(g_shifted, j + 1)
                        nc.scalar.activation(gate[:], gate[:], ACT.Exp).then_inc(g_exp, 1)
                    for hd in range(HEADS):
                        n, nc_, par = j * HEADS + hd, c * HEADS + hd, hd % 2
                        if combine:
                            act.wait_ge(u_used, n * TOPK + (RING + TOPK))
                            if not (first(j) and hd < 2):
                                act.wait_ge(w_ready, n - 1)
                            nc.scalar.activation(act_out[:, par, :], dots[:, par, :], ACT.Gelu_apprx_tanh).then_inc(
                                act_ready, 1
                            )
                        if choose:
                            act.wait_ge(q_ready, nc_ + 1)
                            if not (first(j, -1) and hd < 2):
                                act.wait_ge(s_ready, nc_ - 1)
                            nc.scalar.copy(
                                qT[:, par, :, :], psq[:, par, 0 : 2 * P].rearrange("p (s q) -> p s q", s=2)
                            ).then_inc(q_copied, 1)
                        if combine:
                            act.wait_ge(w_ready, n + 1)
                            for k in range(TOPK):
                                act.wait_ge(v_used, n * TOPK + (k + 1))
                                nc.scalar.activation(
                                    diag[:, k % RING, :], ident[:], ACT.Copy, scale=wgt[:, par, k : k + 1]
                                ).then_inc(diag_ready, 1)

                turns(act, turn)
                if out is not None:
                    for t in range(M):
                        act.wait_ge(x_done, 2 * M)
                        if t:
                            act.wait_ge(fin_sq, t)
                        nc.scalar.activation(
                            V[:, t % 2, :], X[:, T0 + t, :], ACT.Square, accum_out=scores[:, t : t + 1]
                        ).then_inc(fin_sq, 1)
                    act.wait_ge(fin_sq, M)
                    nc.scalar.activation(
                        scores[:, M : 2 * M], scores[:, 0:M], ACT.Sqrt, bias=eps[:, 0:1], scale=1.0 / D
                    ).then_inc(fin_std, 1)

            @block.vector
            def _(dve):
                st = Steps(dve, dve_step)
                dve.sem_inc(u_used, RING)
                dve.wait_ge(const_in, 16 * 9)
                for s in range(2):
                    st.did(
                        nc.vector.scalar_tensor_tensor(
                            out=A[:, s, :], in0=A[:, s, :], scalar=1.0, in1=gain[:], op0=ALU.add, op1=ALU.mult
                        )
                    )
                dve.wait_ge(std_ready, 1)
                st.did(nc.vector.reciprocal(rstd[:], rstd[:]))
                st.restart()
                if out is not None:
                    dve.sem_inc(gain_free, 1)

                def normalise(j, c):
                    x = X[:, bass.ds(c + T0, 1), :].rearrange("p o d -> p (o d)")
                    s = stream(c + T0)
                    a = A[:, bass.ds(s, 1), :].rearrange("p o d -> p (o d)")
                    b = B[:, bass.ds(s, 1), :].rearrange("p o d -> p (o d)")
                    st.then(
                        nc.vector.scalar_tensor_tensor(
                            out=h_next[:], in0=x, scalar=rstd[:, bass.ds(c, 1)], in1=a, op0=ALU.mult, op1=ALU.mult
                        )
                    )
                    st.then(nc.vector.tensor_tensor(h_next[:], h_next[:], b, ALU.add))
                    st.restart()
                    dve.sem_inc(h_ready, 1)

                def shift_gates(j):
                    s3 = scores[:, bass.ds(j * SLOTS, SLOTS)].rearrange("p (h k) -> p h k", h=HEADS)
                    nc.vector.tensor_tensor(
                        gate[:], s3, s3[:, :, 0:1].to_broadcast([P, HEADS, TOPK]), ALU.subtract
                    ).then_inc(g_shifted, 1)

                def finish_gates(j):
                    dve.wait_ge(g_exp, j + 1)
                    st.then(nc.vector.reduce_sum(gsum[:], gate[:], AX))
                    st.then(nc.vector.reciprocal(gsum[:], gsum[:]))
                    st.then(
                        nc.vector.tensor_tensor(
                            gate[:], gate[:], gsum[:].unsqueeze(2).to_broadcast([P, HEADS, TOPK]), ALU.mult
                        )
                    )
                    st.restart()


                def best8_of_halves(w, par):
                    dve.wait_ge(s_ready, w + 1)
                    if not (isinstance(w, int) and w == 0):
                        dve.wait_ge(chosen, w)
                    st.then(nc.vector.tensor_copy(S[:], psS[:, par, 0 : 2 * KEYS].rearrange("p (s k) -> p s k", s=2)))
                    for s in range(2):
                        st.did(nc.vector.max(best[:, s, 0:8], S[:, s, :]))

                def drop_best8():
                    st.settle()
                    for s in range(2):
                        st.did(nc.vector.max_index(ibest[:, s, 0:8], best[:, s, 0:8], S[:, s, :]))
                        st.did(nc.vector.match_replace(S2[:, s, :], best[:, s, 0:8], S[:, s, :], BIG))

                def next8_of_halves():
                    st.settle()
                    for s in range(2):
                        st.did(nc.vector.max(best[:, s, 8:16], S2[:, s, :]))
                    st.settle()
                    for s in range(2):
                        st.did(nc.vector.max_index(ibest[:, s, 8:16], best[:, s, 8:16], S2[:, s, :]))

                c1, c2 = cand[:].rearrange("p a b -> p (a b)"), cand2[:].rearrange("p a b -> p (a b)")

                def best8_of_sums():
                    st.settle()
                    st.then(
                        nc.vector.tensor_tensor(
                            cand[:], best[:, 0, :].unsqueeze(2).to_broadcast([P, TOPK, TOPK]),
                            best[:, 1, :].unsqueeze(1).to_broadcast([P, TOPK, TOPK]), ALU.add,
                        )
                    )
                    st.then(nc.vector.max(top[:, 0:8], c1))
                    st.did(nc.vector.max_index(pos[:, 0:8], top[:, 0:8], c1))
                    st.did(nc.vector.match_replace(c2, top[:, 0:8], c1, BIG))

                def next8_of_sums():
                    st.settle()
                    st.then(nc.vector.max(top[:, 8:16], c2))
                    st.then(nc.vector.max_index(pos[:, 8:16], top[:, 8:16], c2))
                    st.did(nc.vector.tensor_scalar(half_pos[:, 0, :], pos[:], 4, None, ALU.logical_shift_right))
                    st.did(nc.vector.tensor_scalar(half_pos[:, 1, :], pos[:], TOPK - 1, None, ALU.bitwise_and))

                def positions_to_experts(w, hd, tile_0):
                    st.settle()
                    for s in range(2):
                        st.did(
                            nc.vector.tensor_tensor(
                                hot[:, s, :, :], half_pos[:, s, :].unsqueeze(2).to_broadcast([P, TOPK, TOPK]),
                                iota[:].unsqueeze(1).to_broadcast([P, TOPK, TOPK]), ALU.is_equal,
                            )
                        )
                    st.settle()
                    for s in range(2):
                        st.did(
                            nc.vector.tensor_tensor(
                                hot[:, s, :, :], hot[:, s, :, :],
                                ibest[:, s, :].unsqueeze(1).to_broadcast([P, TOPK, TOPK]), ALU.mult,
                            )
                        )
                    st.settle()
                    for s in range(2):
                        st.did(nc.vector.reduce_sum(half_idx[:, s, :], hot[:, s, :, :], AX))
                    st.then(nc.vector.tensor_copy(scores[:, bass.ds(w * TOPK, TOPK)], top[:]))
                    st.restart()
                    if not tile_0:
                        dve.wait_ge(idx_copied, (w - HEADS) * TOPK + TOPK)
                    nc.vector.scalar_tensor_tensor(
                        out=experts[:, hd * TOPK : (hd + 1) * TOPK], in0=half_idx[:, 0, :], scalar=float(KEYS), in1=half_idx[:, 1, :],
                        op0=ALU.mult, op1=ALU.add,
                    ).then_inc(chosen, 1)

                def choice_step(step, w, hd, tile_0):
                    if step == 0:
                        best8_of_halves(w, hd % 2)
                    elif step == 1:
                        drop_best8()
                    elif step == 2:
                        next8_of_halves()
                    elif step == 3:
                        best8_of_sums()
                    elif step == 4:
                        next8_of_sums()
                    else:
                        positions_to_experts(w, hd, tile_0)

                def add_tile(j):
                    t = j + T0
                    g = g2[:, bass.ds(stream(t), 1), :].rearrange("p o d -> p (o d)")
                    x = X[:, bass.ds(t, 1), :].rearrange("p o d -> p (o d)")
                    for h in range(2):
                        cols = slice(512 * h, 512 * h + 512)
                        dve.wait_ge(y_ready, j + 1)
                        if h:
                            dve.wait_ge(x_done, j * 2 + 1)
                        st.then(nc.vector.tensor_tensor(h_tmp[:, cols], psY[:, cols], g[:, cols], ALU.mult))
                        st.restart()
                        nc.vector.tensor_tensor(x[:, cols], x[:, cols], h_tmp[:, cols], ALU.add).then_inc(x_done, 1)
                    dve.sem_inc(y_taken, 1)

                def turn(j, choose, combine):
                    c = j + 1
                    if combine:
                        st.then(nc.vector.tensor_copy(h_cur[:], h_next[:]))
                        st.restart()
                    if choose:
                        normalise(j, c)
                    for hd in range(HEADS):
                        n, par = j * HEADS + hd, hd % 2
                        w, w_hd, w_tile_0 = c * HEADS + hd - 1, (hd - 1) % HEADS, first(j, -1) or (first(j) and hd == 0)
                        choosing = (choose or hd == 0) and not (first(j, -1) and hd == 0)
                        if choosing and not combine:
                            for step in range(6):
                                choice_step(step, w, w_hd, w_tile_0)
                        if combine:
                            if not (first(j) and hd < 2):
                                dve.wait_ge(act_ready, n - 1)
                            for k in range(TOPK):
                                r = k % RING
                                dve.wait_ge(u_in[r], n * (16 * TOPK // RING) + 16 * (k // RING + 1))
                                nc.vector.tensor_tensor_reduce(
                                    U[:, r, :], U[:, r, :], h_cur[:], 1.0, 0.0, ALU.mult, ALU.add,
                                    dots[:, par, k : k + 1],
                                ).then_inc(u_used, 1)
                                if choosing and k % 2 == 1 and k < 12:
                                    choice_step(k // 2, w, w_hd, w_tile_0)
                            if hd == 0:
                                shift_gates(j)
                                if not first(j):
                                    add_tile(j - 1)
                                finish_gates(j)
                            dve.wait_ge(act_ready, n + 1)
                            if not (first(j) and hd < 2):
                                dve.wait_ge(diag_ready, n * TOPK - TOPK)
                            nc.vector.tensor_tensor(wgt[:, par, :], act_out[:, par, :], gate[:, hd, :], ALU.mult).then_inc(
                                w_ready, 1
                            )

                turns(dve, turn)
                add_tile(M - 1)
                if out is not None:
                    dve.wait_ge(fin_std, 1)
                    dve.wait_ge(gain_in, 16)
                    st.then(nc.vector.reciprocal(scores[:, 2 * M : 3 * M], scores[:, M : 2 * M]))
                    for t in range(M):
                        nc.vector.scalar_tensor_tensor(
                            out=X[:, T0 + t, :], in0=X[:, T0 + t, :], scalar=scores[:, 2 * M + t : 2 * M + t + 1],
                            in1=gain[:], op0=ALU.mult, op1=ALU.mult,
                        ).then_inc(fin_done, 1)

            @block.tensor
            def _(pe):
                pe.sem_inc(v_used, RING)
                pe.wait_ge(wq_in, 16)
                pe.wait_ge(const_in, 16 * 9)

                def turn(j, choose, combine):
                    c = j + 1
                    if choose:
                        pe.wait_ge(h_ready, c + 1)
                        for k in range(DC):
                            ins = nc.tensor.transpose(psT[:, k * P : (k + 1) * P], h_next[:, k * P : (k + 1) * P], ident[:])
                        ins.then_inc(tr_ready, 1)
                        pe.wait_ge(hT_ready, c * 2 + 2)
                    for hd in range(HEADS):
                        n, nc_, par = j * HEADS + hd, c * HEADS + hd, hd % 2
                        if choose:
                            if not (first(j, -1) and hd < 2):
                                pe.wait_ge(q_copied, nc_ - 1)
                            for s in range(2):
                                c0 = (2 * hd + s) * P
                                for k in range(DC):
                                    ins = nc.tensor.matmul(
                                        psq[:, par, s * P : (s + 1) * P], wq[:, k, c0 : c0 + P], hT[:, k, :],
                                        start=(k == 0), stop=(k == DC - 1),
                                    )
                            ins.then_inc(q_ready, 1)
                            pe.wait_ge(q_copied, nc_ + 1)
                            if not (first(j, -1) and hd < 2):
                                pe.wait_ge(chosen, nc_ - 1)
                            for s in range(2):
                                ins = nc.tensor.matmul(
                                    psS[:, par, s * KEYS : (s + 1) * KEYS], qT[:, par, s, :], keys[:, 2 * hd + s, :],
                                    start=True, stop=True,
                                )
                            ins.then_inc(s_ready, 1)
                        if combine:
                            if hd == 0 and not first(j):
                                pe.wait_ge(y_taken, j)
                            for k in range(TOPK):
                                r = k % RING
                                pe.wait_ge(diag_ready, n * TOPK + (k + 1))
                                pe.wait_ge(v_in[r], n * (16 * TOPK // RING) + 16 * (k // RING + 1))
                                for h in range(2):
                                    cols = slice(512 * h, 512 * h + 512)
                                    ins = nc.tensor.matmul(
                                        psY[:, cols], diag[:, r, :], V[:, r, cols],
                                        start=(hd == 0 and k == 0), stop=(hd == HEADS - 1 and k == TOPK - 1),
                                    )
                                ins.then_inc(v_used, 1)
                            if hd == HEADS - 1:
                                pe.wait_ge(v_used, n * TOPK + (RING + TOPK))
                                pe.sem_inc(y_ready, 1)

                turns(pe, turn)




def mixer_rg_stage(nc, io, mod_dram, X, ident, eps):
    with ExitStack() as outer:
        mo = Pool(nc, outer, "rg")
        XC = mo.sb("XC", [P, RB, XCW])
        G = mo.sb("G", [P, RB, SEQ])
        wg = mo.sb("wg", [P, 4, RB, P])
        g1 = mo.sb("g1", [P, D])
        cl = mo.sb("cl", [P, 2, RB])
        ba, bx = mo.sb("ba", [P, 2, RB]), mo.sb("bx", [P, 2, RB])
        rg_input_part(nc, io, mod_dram, X, ident, eps, XC, G, wg, g1, cl, ba, bx)
        rg_scan_part(nc, io, X, XC, G, wg, g1, cl, ba, bx)


def rg_input_part(nc, io, mod_dram, X, ident, eps, XC, G, wg, g1, cl, ba, bx):
    RING = 6
    with ExitStack() as ctx:
        m = Pool(nc, ctx, "rgi")
        normbc = m.sb("normbc", [P, 5 * D])
        hN = m.sb("hN", [P, 2, D])
        hT = m.sb("hT", [P, DC, TOK])
        W = m.sb("W", [P, RING, DC, P])
        raw = m.sb("raw", [P, 2, RAWW])
        cw, cb = m.sb("cw", [P, RB, CONV]), m.sb("cb", [P, RB])
        lam = m.sb("lam", [P, 2, RB])
        e1, z, z2, poly = (m.sb(x, [P, 2, RB]) for x in ("e1", "z", "z2", "poly"))
        TR = m.ps("TR", [P, 2, D])
        MM = m.ps("MM", [P, 4, 512])
        norm = NormTranspose(m, X, ident, G[:, 0:2, :].rearrange("p a b -> p (a b)"), normbc, hT, hN, TR)
        norm.eps = eps
        w_in = [m.sem(f"w_in{r}") for r in range(RING)]
        small_in, late_in = m.sem("small_in"), m.sem("late_in")
        mm_ready, mm_free, conv_done, dve_step, e_ready = (
            m.sem(x) for x in ("mm_ready", "mm_free", "conv_done", "dve_step", "e_ready")
        )
        block_done, zeros, abs_ready, act_step = m.sem("block_done"), m.sem("zeros"), m.sem("abs_ready"), m.sem("act_step")
        NB = 2 * RB

        with nc.Block() as block:

            @block.sync
            def _(sp):
                norm.load(nc, sp, io, mod_dram, 1)
                for dst, src in (
                    (cw[:], io["conv_wT"]), (cb[:], io["conv_bT"]), (lam[:], io["rg_lambdaT"]),
                    (ba[:], io["rg_baT"]), (bx[:], io["rg_bxT"]),
                ):
                    sp.dma_start(dst, src).then_inc(small_in, 16)
                w = io["rg_w_in"][0].rearrange("(c p) n -> p c n", p=P)
                for b in range(NB):
                    c0 = DR + b * P if b < RB else (b - RB) * P
                    if b >= RING:
                        sp.wait_ge(block_done, b - RING + 1)
                    sp.dma_start(W[:, b % RING, :, :], w[:, :, c0 : c0 + P]).then_inc(w_in[b % RING], 16)
                sp.dma_start(wg[:], io["rg_gatesT"]).then_inc(late_in, 16)
                sp.dma_start(g1[:], mod_dram[1, 1, 2].partition_broadcast(P)).then_inc(late_in, 16)
                sp.wait_ge(late_in, 32)

            @block.scalar
            def _(act):
                norm.scalar_sums(nc, act, lambda e, t: None)
                norm.scalar_out(nc, act)
                act.wait_ge(zeros, 1)
                for b in range(RB):
                    if b >= 2:
                        act.wait_ge(conv_done, b - 1)
                    for part, (r0, n) in enumerate(((RAW_CTX, CTX), (RAW_LAT, SEQ))):
                        job = 2 * b + part
                        act.wait_ge(mm_ready, job + 1)
                        nc.scalar.copy(raw[:, b % 2, r0 : r0 + n], MM[:, job % 4, 0:n]).then_inc(mm_free, 1)
                act.wait_ge(abs_ready, 1)
                nc.scalar.activation(e1[:], z[:], ACT.Exp, scale=-1.0).then_inc(e_ready, 1)
                for b in range(RB):
                    job = 2 * RB + b
                    act.wait_ge(mm_ready, job + 1)
                    nc.scalar.activation(G[:, b, :], MM[:, job % 4, :], ACT.Gelu_apprx_tanh).then_inc(mm_free, 1)

            @block.vector
            def _(dve):
                st = Steps(dve, dve_step)
                nc.vector.memset(raw[:], 0.0).then_inc(zeros, 1)
                norm.vector(nc, dve, st)
                dve.wait_ge(small_in, 16 * 5)
                for b in range(RB):
                    y, x = XC[:, b, :], raw[:, b % 2, :]
                    dve.wait_ge(mm_free, 2 * b + 2)
                    dve.wait_ge(zeros, 1)
                    st.then(nc.vector.tensor_scalar(y, x[:, 0:XCW], cw[:, b, 0:1], cb[:, b : b + 1], ALU.mult, ALU.add))
                    for j in range(1, CONV):
                        ins = nc.vector.scalar_tensor_tensor(
                            out=y, in0=x[:, j : j + XCW], scalar=cw[:, b, j : j + 1], in1=y, op0=ALU.mult, op1=ALU.add
                        )
                        if j < CONV - 1:
                            st.then(ins)
                    ins.then_inc(conv_done, 1)
                st.then(nc.vector.tensor_scalar(z[:], lam[:], -1.0, None, ALU.mult))
                st.then(nc.vector.tensor_tensor(z[:], z[:], lam[:], ALU.max))
                dve.sem_inc(abs_ready, 1)
                dve.wait_ge(e_ready, 1)
                st.then(nc.vector.tensor_scalar(z2[:], e1[:], 2.0, None, ALU.add))
                st.then(nc.vector.reciprocal(z2[:], z2[:]))
                st.then(nc.vector.tensor_tensor(z[:], e1[:], z2[:], ALU.mult))
                st.then(nc.vector.tensor_tensor(z2[:], z[:], z[:], ALU.mult))
                st.then(nc.vector.memset(poly[:], 1.0 / 17.0))
                for k in range(7, -1, -1):
                    st.then(nc.vector.tensor_tensor(poly[:], poly[:], z2[:], ALU.mult))
                    st.then(nc.vector.tensor_scalar(poly[:], poly[:], 1.0 / (2 * k + 1), None, ALU.add))
                st.then(nc.vector.tensor_tensor(poly[:], poly[:], z[:], ALU.mult))
                st.then(nc.vector.tensor_scalar(e1[:], lam[:], -1.0, 0.0, ALU.mult, ALU.max))
                st.then(
                    nc.vector.scalar_tensor_tensor(out=z[:], in0=poly[:], scalar=2.0, in1=e1[:], op0=ALU.mult, op1=ALU.add)
                )
                st.then(nc.vector.tensor_scalar(cl[:], z[:], -4.0, None, ALU.mult))

            @block.tensor
            def _(pe):
                norm.tensor(nc, pe)
                pe.wait_ge(norm.hT_ready, 2 * NT)
                for b in range(NB):
                    pe.wait_ge(w_in[b % RING], 16 * (b // RING + 1))
                    parts = ((0, CTX), (CTX, TOK)) if b < RB else ((CTX, TOK),)
                    for part, (a0, a1) in enumerate(parts):
                        job = 2 * b + part if b < RB else RB + b
                        if job >= 4:
                            pe.wait_ge(mm_free, job - 3)
                        for k in range(DC):
                            ins = nc.tensor.matmul(
                                MM[:, job % 4, 0 : a1 - a0], W[:, b % RING, k, :], hT[:, k, a0:a1],
                                start=(k == 0), stop=(k == DC - 1),
                            )
                        ins.then_inc(mm_ready, 1)
                    pe.wait_ge(mm_ready, job + 1)
                    pe.sem_inc(block_done, 1)


def rg_scan_part(nc, io, X, XC, G, wg, g1, cl, ba, bx):
    NBG = 5
    NGROUP = RB // NBG
    with ExitStack() as ctx:
        m = Pool(nc, ctx, "rgs")
        A = m.sb("A", [P, NBG, XCW])
        big = m.sb("big", [P, 2, NBG, XCW])
        Mm, IX = big[:, 0, :, :], big[:, 1, :, :]
        Dd = m.sb("Dd", [P, 2, XCW])
        scan_ctx = m.sb("scan_ctx", [P, 2, CTX])
        back = m.sb("back", [P, 2, SEQ])
        HF = m.sb("HF", [P, NBG, SEQ])
        Wh = m.sb("Wh", [P, RB, 512])
        ps = m.ps("ps", [P, 2, 2, 2, 512])
        r_ready, r_taken, i_taken, th_ready, a_ready, m_ready, sqrt_ready, scanned = (
            m.sem(x)
            for x in ("r_ready", "r_taken", "i_taken", "th_ready", "a_ready", "m_ready", "sqrt_ready", "scanned")
        )
        sum_done, y_done, out_ready, x_done, dve_step, w_in, w_free = (
            m.sem(x) for x in ("sum_done", "y_done", "out_ready", "x_done", "dve_step", "w_in", "w_free")
        )
        units = [(g * NBG + i, d) for g in range(NGROUP) for d in range(2) for i in range(NBG)]

        with nc.Block() as block:

            @block.sync
            def _(sp):
                w = io["rg_w_out"][0].rearrange("(c p) n -> p c n", p=P)
                for h in range(2):
                    if h:
                        sp.wait_ge(out_ready, LT)
                    sp.dma_start(Wh[:], w[:, :, 512 * h : 512 * h + 512]).then_inc(w_in, 16)

            @block.tensor
            def _(pe):
                for u, (b, d) in enumerate(units):
                    if u >= 2:
                        pe.wait_ge(i_taken, u - 1)
                        pe.wait_ge(r_taken, u - 1)
                    for k in range(2):
                        for h in range(2):
                            ins = nc.tensor.matmul(
                                ps[:, u % 2, k, h, 0:HALF], wg[:, 2 * k + d, b, :], XC[:, b, h * HALF : (h + 1) * HALF],
                                start=True, stop=True,
                            )
                    ins.then_inc(r_ready, 1)
                pe.wait_ge(y_done, RB)
                pe.wait_ge(i_taken, len(units))
                for h in range(2):
                    pe.wait_ge(w_in, 16 * (h + 1))
                    for t in range(LT):
                        n = h * LT + t
                        if n >= 4:
                            pe.wait_ge(x_done, n - 3)
                        for k in range(RB):
                            ins = nc.tensor.matmul(
                                ps[:, n % 4 // 2, n % 2, 0, :], G[:, k, t * P : (t + 1) * P], Wh[:, k, :],
                                start=(k == 0), stop=(k == RB - 1),
                            )
                        ins.then_inc(out_ready, 1)

            @block.scalar
            def _(act):
                for g0 in range(0, len(units), NBG):
                    for i in range(NBG):
                        u = g0 + i
                        b, d = units[u]
                        act.wait_ge(r_ready, u + 1)
                        if u >= NBG:
                            act.wait_ge(scanned, u - NBG + 1)
                        nc.scalar.activation(
                            Mm[:, i, :].rearrange("p (a k) -> p a k", a=2), ps[:, u % 2, 0, :, 0:HALF], ACT.Sigmoid,
                            bias=ba[:, d, b : b + 1],
                        ).then_inc(r_taken, 1)
                        nc.scalar.activation(
                            IX[:, i, :].rearrange("p (a k) -> p a k", a=2), ps[:, u % 2, 1, :, 0:HALF], ACT.Sigmoid,
                            bias=bx[:, d, b : b + 1],
                        ).then_inc(i_taken, 1)
                        act.wait_ge(r_taken, u + 1)
                        nc.scalar.activation(Mm[:, i, :], Mm[:, i, :], ACT.Tanh, scale=cl[:, d, b : b + 1]).then_inc(
                            th_ready, 1
                        )
                    for i in range(NBG):
                        u = g0 + i
                        act.wait_ge(m_ready, u + 1)
                        nc.scalar.activation(Mm[:, i, :], Mm[:, i, :], ACT.Sqrt).then_inc(sqrt_ready, 1)

            @block.gpsimd
            def _(pool):
                for u, (b, d) in enumerate(units):
                    i = u % NBG
                    pool.wait_ge(i_taken, u + 1)
                    nc.gpsimd.tensor_tensor(IX[:, i, :], IX[:, i, :], XC[:, b, :], ALU.mult).then_inc(a_ready, 1)

            @block.vector
            def _(dve):
                st = Steps(dve, dve_step)

                def decay(u):
                    i = u % NBG
                    th, dd, a = Mm[:, i, :], Dd[:, u % 2, :], A[:, i, :]
                    dve.wait_ge(th_ready, u + 1)
                    st.then(nc.vector.tensor_scalar(dd, th, -1.0, 1.0, ALU.mult, ALU.add))
                    st.then(nc.vector.reciprocal(dd, dd))
                    st.did(nc.vector.scalar_tensor_tensor(out=a, in0=th, scalar=1.0, in1=dd, op0=ALU.add, op1=ALU.mult))
                    st.then(nc.vector.scalar_tensor_tensor(out=dd, in0=th, scalar=-2.0, in1=dd, op0=ALU.mult, op1=ALU.mult))
                    nc.vector.scalar_tensor_tensor(out=th, in0=a, scalar=1.0, in1=dd, op0=ALU.add, op1=ALU.mult).then_inc(
                        m_ready, 1
                    )

                def scan(u):
                    b, d = units[u]
                    i = u % NBG
                    dve.wait_ge(sqrt_ready, u + 1)
                    dve.wait_ge(a_ready, u + 1)
                    st.then(nc.vector.tensor_tensor(Mm[:, i, :], Mm[:, i, :], IX[:, i, :], ALU.mult))
                    c, lat = slice(OUT_CTX, OUT_CTX + CTX), slice(OUT_LAT, OUT_LAT + SEQ)
                    ac, uc, al, ul = A[:, i, c], Mm[:, i, c], A[:, i, lat], Mm[:, i, lat]
                    sc, out = scan_ctx[:, u % 2, :], HF[:, i, :] if d == 0 else back[:, u % 2, :]
                    if d == 0:
                        st.then(nc.vector.tensor_tensor_scan(sc, ac, uc, 0.0, ALU.mult, ALU.add))
                        ins = nc.vector.tensor_tensor_scan(out, al, ul, sc[:, CTX - 1 : CTX], ALU.mult, ALU.add)
                    else:
                        st.then(nc.vector.tensor_tensor_scan(sc[:, ::-1], ac[:, ::-1], uc[:, ::-1], 0.0, ALU.mult, ALU.add))
                        ins = nc.vector.tensor_tensor_scan(
                            out[:, ::-1], al[:, ::-1], ul[:, ::-1], sc[:, 0:1], ALU.mult, ALU.add
                        )
                    ins.then_inc(scanned, 1)
                    if d == 1:
                        dve.wait_ge(scanned, u + 1)
                        st.then(nc.vector.tensor_tensor(out, out, HF[:, i, :], ALU.add))
                        nc.vector.tensor_tensor(G[:, b, :], G[:, b, :], out, ALU.mult).then_inc(y_done, 1)

                for g0 in range(0, len(units), NBG):
                    for i in range(NBG):
                        decay(g0 + i)
                    for i in range(NBG):
                        scan(g0 + i)
                tmp = scan_ctx[:].rearrange("p a b -> p (a b)")
                for n in range(2 * LT):
                    h, t = n // LT, n % LT
                    cols = slice(512 * h, 512 * h + 512)
                    dve.wait_ge(out_ready, n + 1)
                    if n:
                        dve.wait_ge(x_done, n)
                    st.then(nc.vector.tensor_tensor(tmp, ps[:, n % 4 // 2, n % 2, 0, :], g1[:, cols], ALU.mult))
                    x = X[:, CT + t, cols]
                    nc.vector.tensor_tensor(x, x, tmp, ALU.add).then_inc(x_done, 1)




def constants():
    n = np.arange(SEQ)
    freq = (10000.0 ** (-np.arange(HD // 4, dtype=np.float32) / (HD // 4))).astype(np.float32)
    ang = np.stack([(n // GRID_W).astype(np.float32)[:, None] * freq, (n % GRID_W).astype(np.float32)[:, None] * freq], 1)
    cos = np.ones((HD, TOK), np.float32)
    sin = np.zeros((HD, TOK), np.float32)
    rot = np.zeros((HD, HD), np.float32)
    f = HD // 4
    for axis in range(2):
        for half in range(2):
            a = axis * 2 * f + half * f
            cos[a : a + f, CTX:] = np.cos(ang[:, axis]).T
            sin[a : a + f, CTX:] = np.sin(ang[:, axis]).T
            b = axis * 2 * f + (1 - half) * f
            rot[b + np.arange(f), a + np.arange(f)] = -1.0 if half == 0 else 1.0
    return {
        "cos": cos, "sin": sin, "rotm": rot, "ident": np.eye(P, dtype=np.float32),
        "iota": np.tile(np.arange(TOPK, dtype=np.float32), (P, 1)),
    }


def constants_stage(nc, io, ident, ones, eps):
    with ExitStack() as ctx:
        m = Pool(nc, ctx, "const")
        const_in = m.sem("const_in")
        with nc.Block() as block:

            @block.sync
            def _(sp):
                sp.dma_start(ident[:], io["ident"]).then_inc(const_in, 16)
                sp.wait_ge(const_in, 16)

            @block.vector
            def _(dve):
                nc.vector.memset(ones[:], 1.0)
                nc.vector.memset(eps[:], EPS)


def trunk(nc, io, out, upto=5):
    mod_dram = nc.dram_tensor("modulation", (2, 2, 6, D), F32, kind="Internal").ap()
    with ExitStack() as ctx:
        m = Pool(nc, ctx, "all")
        ident, ones, eps = m.sb("ident", [P, P]), m.sb("ones", [P, P]), m.sb("eps", [P, 1])
        constants_stage(nc, io, ident, ones, eps)
        modulation_stage(nc, io, mod_dram)
        X = m.sb("X", [P, NT, D])
        mixer_ab_stage(nc, io, mod_dram, X, ident, ones, eps)
        if upto >= 2:
            peer_stage(nc, io, mod_dram, X, ident, eps, 0, 0, None)
        if upto >= 3:
            mixer_rg_stage(nc, io, mod_dram, X, ident, eps)
        if upto >= 4:
            peer_stage(nc, io, mod_dram, X, ident, eps, 1, CT, out)
        else:
            dump(nc, X, out)


def dump(nc, X, out):
    with nc.semaphore("dumped") as s, nc.Block() as block:

        @block.sync
        def _(sp):
            sp.dma_start(out.rearrange("(t p) d -> p t d", p=P), X[:]).then_inc(s, 16)
            sp.wait_ge(s, 16)


def layouts(inp):
    f = lambda a: np.ascontiguousarray(a)
    io = {
        n: f(inp[n])
        for n in (
            "x", "c", "ctx", "c_ctx", "mod_w", "mod_b", "norm1_g", "norm2_g", "ab_w_in", "gmlp_bs", "ab_w_out",
            "rg_w_in", "rg_w_out", "peer_wq", "final_norm_g",
        )
    }
    io["wsT"] = f(inp["gmlp_ws"][0].transpose(2, 0, 1))
    io["gmlp_gT"] = f(inp["gmlp_norm_g"][0].reshape(GROUPS, P).T)
    io["qk_gT"] = f(np.stack([inp["q_norm_g"][0], inp["k_norm_g"][0]], 1))
    for layer in range(2):
        io[f"peer_u{layer}"] = f(inp["peer_u"][layer])
        io[f"peer_v{layer}"] = f(inp["peer_v"][layer])
    io["keysT"] = f(inp["peer_keys"].transpose(0, 4, 1, 2, 3).reshape(2, P, 2 * HEADS, KEYS))
    io["conv_wT"] = f(inp["rg_conv_w"][0].reshape(CONV, RB, P).transpose(2, 1, 0))
    io["conv_bT"] = f(inp["rg_conv_b"][0].reshape(RB, P).T)
    gates = np.concatenate([inp["rg_wa"][0], inp["rg_wx"][0]])
    io["rg_gatesT"] = f(gates.transpose(2, 0, 1, 3))
    for n in ("rg_ba", "rg_bx", "rg_lambda"):
        io[n + "T"] = f(inp[n][0].reshape(2, RB, P).transpose(2, 0, 1))
    io.update(constants())
    return io


def kernel(**inputs):
    import concourse.bacc as bacc
    from concourse.bass_utils import run_bass_kernel_spmd

    arrays = layouts({n: np.asarray(a) for n, a in inputs.items()})
    nc = bacc.Bacc("TRN2", target_bir_lowering=False, num_devices=1)
    io = {
        n: nc.dram_tensor("in_" + n, a.shape, mybir.dt.from_np(a.dtype), kind="ExternalInput").ap()
        for n, a in arrays.items()
    }
    out = nc.dram_tensor("out", (1, SEQ, D), F32, kind="ExternalOutput").ap()
    trunk(nc, io, out)
    got = run_bass_kernel_spmd(nc, [{"in_" + n: a for n, a in arrays.items()}], core_ids=[0])
    return got.results[0]["out"]
```

```python
from contextlib import ExitStack

import numpy as np

import concourse.bass as bass
from concourse import mybir

ALU = mybir.AluOpType
ACT = mybir.ActivationFunctionType
AX = mybir.AxisListType.X
F32 = mybir.dt.float32
U32 = mybir.dt.uint32

P = 128
D = 1024
DC = D // P
SEQ, CTX = 512, 256
CT, LT = CTX // P, SEQ // P
NT = CT + LT
TOK = NT * P
EPS = 1e-6
GRID_W = 64
HD = 128
NQ, NKV = 4, 2
NQK = NQ + NKV
GROUPS = 4
AW = GROUPS * P
DR = 1280
RB = DR // P
CONV = 4
HEADS = 8
KEYS = 128
TOPK = 16
SLOTS = HEADS * TOPK
BIG = -3.0e38
RAW_CTX, RAW_LAT = 2, 2 + CTX + 1 + 2
OUT_CTX, OUT_LAT = RAW_CTX - 2, RAW_LAT - 2
XCW = OUT_LAT + SEQ + 1
HALF = XCW // 2
RAWW = XCW + CONV - 1


def stream(t):
    return (t + LT - CT) // LT


class Steps:

    def __init__(self, eng, sem):
        self.eng, self.sem, self.n = eng, sem, 0

    def did(self, ins):
        ins.then_inc(self.sem, 1)
        self.n += 1
        return self.n

    def settle(self):
        self.eng.wait_ge(self.sem, self.n)

    def then(self, ins):
        self.did(ins)
        self.settle()

    def restart(self):
        self.settle()
        self.eng.sem_clear(self.sem)
        self.n = 0


class Pool:

    def __init__(self, nc, ctx, stage):
        self.nc, self.ctx, self.stage = nc, ctx, stage
        self.sems = []
        ctx.callback(self.clear)

    def sb(self, name, shape, dt=F32):
        return self.ctx.enter_context(self.nc.sbuf_tensor(f"{self.stage}_{name}", shape, dt))

    def ps(self, name, shape):
        return self.ctx.enter_context(self.nc.psum_tensor(f"{self.stage}_{name}", shape, F32))

    def sem(self, name):
        self.sems.append(self.nc.alloc_semaphore(f"{self.stage}_{name}"))
        return self.sems[-1]

    def clear(self):
        if self.sems:
            with self.nc.Block() as block:

                @block.gpsimd
                def _(pool):
                    self.nc.clear_and_free_semaphores(self.sems)




def modulation_stage(nc, io, mod_dram, X, x_in):
    CW = 512
    NCH = 2 * 6 * D // CW
    RING = 4
    TURNS = NCH // RING
    with ExitStack() as ctx:
        m = Pool(nc, ctx, "mod")
        cv = m.sb("cv", [P, 2, DC])
        sg = m.sb("sg", [P, 2, DC])
        sT = m.sb("sT", [P, 2, DC])
        W = m.sb("W", [P, RING, DC, CW])
        sums = m.sb("sums", [P, 2, CW])
        pick = m.sb("pick", [P, 2, 2])
        bias = m.sb("bias", [2, 12 * D])
        acc = m.ps("acc", [P, RING, CW])
        c_in, bias_in = m.sem("c_in"), m.sem("bias_in")
        w_in = [m.sem(f"w_in{r}") for r in range(RING)]
        chunk_done, sums_ready, sums_used = m.sem("chunk_done"), m.sem("sums_ready"), m.sem("sums_used")
        sig_ready, s_ready, pick_ready = m.sem("sig_ready"), m.sem("s_ready"), m.sem("pick_ready")
        acc_free, stored, dve_step = m.sem("acc_free"), m.sem("stored"), m.sem("dve_step")

        with nc.Block() as block:

            @block.sync
            def _(sp):
                sp.dma_start(cv[:, 0, :], io["c_ctx"].rearrange("(p k) -> p k", k=DC)).then_inc(c_in, 16)
                sp.dma_start(cv[:, 1, :], io["c"].rearrange("a (p k) -> p (a k)", k=DC)).then_inc(c_in, 16)
                sp.dma_start(bias[:], io["mod_b"].rearrange("l n -> (l n)").partition_broadcast(2)).then_inc(
                    bias_in, 16
                )
                for layer in range(2):
                    w = io["mod_w"][layer].rearrange("(p k) n -> p k n", k=DC)
                    with sp.Fori(0, TURNS // 2) as i:
                        g = i + layer * (TURNS // 2)
                        for r in range(RING):
                            if r == 0:
                                sp.wait_ge(sums_ready, g + 1)
                            else:
                                sp.wait_ge(chunk_done, g * (RING - 1) + r)
                            sp.dma_start(W[:, r, :, :], w[:, :, bass.ds((i * RING + r) * CW, CW)]).then_inc(w_in[r], 16)
                for t in range(NT):
                    src = io["ctx"][0, t * P : (t + 1) * P, :] if t < CT else io["x"][0, (t - CT) * P : (t - CT + 1) * P, :]
                    sp.dma_start(X[:, t, :], src).then_inc(x_in[t], 16)
                sp.wait_ge(acc_free, RING + NCH)
                sp.dma_start(mod_dram.rearrange("s l j d -> s (l j d)"), bias[:]).then_inc(stored, 16)
                sp.wait_ge(stored, 16)

            @block.scalar
            def _(act):
                act.wait_ge(c_in, 32)
                nc.scalar.activation(sg[:], cv[:], ACT.Sigmoid).then_inc(sig_ready, 1)

            @block.vector
            def _(dve):
                st = Steps(dve, dve_step)
                dve.sem_inc(acc_free, RING)
                dve.sem_inc(sums_ready, 1)
                st.then(nc.vector.memset(pick[:], 0.0))
                for s in range(2):
                    st.did(nc.vector.memset(pick[:, s, s : s + 1], 1.0))
                st.restart()
                dve.sem_inc(pick_ready, 1)
                dve.wait_ge(sig_ready, 1)
                nc.vector.tensor_tensor(sT[:], sg[:], cv[:], ALU.mult).then_inc(s_ready, 1)
                dve.wait_ge(s_ready, 1)
                dve.wait_ge(bias_in, 16)
                with dve.Fori(0, TURNS) as i:
                    dve.wait_ge(w_in[0], i * 16 + 16)
                    dve.wait_ge(sums_used, i + 1)
                    for s in range(2):
                        st.did(nc.vector.tensor_scalar(sums[:, s, :], W[:, 0, 0, :], sT[:, s, 0:1], None, ALU.mult))
                    for k in range(1, DC):
                        st.settle()
                        for s in range(2):
                            st.did(
                                nc.vector.scalar_tensor_tensor(
                                    out=sums[:, s, :], in0=W[:, 0, k, :], scalar=sT[:, s, k : k + 1], in1=sums[:, s, :],
                                    op0=ALU.mult, op1=ALU.add,
                                )
                            )
                    st.restart()
                    dve.sem_inc(sums_ready, 1)
                    for r in (1, 2, 3, 0):
                        if r:
                            dve.wait_ge(chunk_done, i * (RING - 1) + (RING - 1 + r))
                        else:
                            dve.wait_ge(sums_used, i + 2)
                        cols = bass.ds((i * RING + r) * CW, CW)
                        nc.vector.tensor_tensor(bias[:, cols], acc[0:2, r, :], bias[:, cols], ALU.add).then_inc(
                            acc_free, 1
                        )

            @block.tensor
            def _(pe):
                pe.sem_inc(chunk_done, RING - 1)
                pe.sem_inc(sums_used, 1)
                pe.wait_ge(s_ready, 1)
                pe.wait_ge(pick_ready, 1)
                with pe.Fori(0, TURNS) as i:
                    for n, r in enumerate((1, 2, 3, 0)):
                        if r:
                            pe.wait_ge(w_in[r], i * 16 + 16)
                        else:
                            pe.wait_ge(sums_ready, i + 2)
                        pe.wait_ge(acc_free, i * RING + (n + 1))
                        if r:
                            for k in range(DC):
                                ins = nc.tensor.matmul(
                                    acc[0:2, r, :], sT[:, :, k], W[:, r, k, :], start=(k == 0), stop=(k == DC - 1)
                                )
                            ins.then_inc(chunk_done, 1)
                        else:
                            for s in range(2):
                                ins = nc.tensor.matmul(
                                    acc[0:2, r, :], pick[:, s, :], sums[:, s, :], start=(s == 0), stop=(s == 1)
                                )
                            ins.then_inc(sums_used, 1)




class NormTranspose:

    def __init__(self, m, X, ident, junk, normbc, hT, hN, TR):
        self.X, self.ident, self.junk, self.hT, self.hN, self.TR = X, ident, junk, hT, hN, TR
        self.A = normbc[:, 0 : 2 * D].rearrange("p (s d) -> p s d", s=2)
        self.B = normbc[:, 2 * D : 4 * D].rearrange("p (s d) -> p s d", s=2)
        self.gain = normbc[:, 4 * D : 5 * D]
        self.ss = m.sb("ss", [P, NT])
        self.std = m.sb("std", [P, NT])
        self.rstd = m.sb("rstd", [P, NT])
        self.mod_in, self.sq_done, self.std_ready = m.sem("mod_in"), m.sem("sq_done"), m.sem("std_ready")
        self.h_ready, self.tr_ready, self.hT_ready = m.sem("h_ready"), m.sem("tr_ready"), m.sem("hT_ready")

    def load(self, nc, sp, io, mod_dram, layer):
        for s in range(2):
            sp.dma_start(self.A[:, s, :], mod_dram[s, layer, 1].partition_broadcast(P)).then_inc(self.mod_in, 16)
            sp.dma_start(self.B[:, s, :], mod_dram[s, layer, 0].partition_broadcast(P)).then_inc(self.mod_in, 16)
        sp.dma_start(self.gain, io["norm1_g"][layer].partition_broadcast(P)).then_inc(self.mod_in, 16)

    def scalar_sums(self, nc, act, x_wait):
        for t in range(NT):
            x_wait(act, t)
            if t:
                act.wait_ge(self.sq_done, t)
            nc.scalar.activation(
                self.junk, self.X[:, t, :], ACT.Square, accum_out=self.ss[:, t : t + 1]
            ).then_inc(self.sq_done, 1)
        act.wait_ge(self.sq_done, NT)
        nc.scalar.activation(self.std[:], self.ss[:], ACT.Sqrt, bias=self.eps[:, 0:1], scale=1.0 / D).then_inc(self.std_ready, 1)

    def scalar_out(self, nc, act, tiles=range(NT)):
        for t in tiles:
            act.wait_ge(self.tr_ready, t + 1)
            for h in range(2):
                nc.scalar.copy(
                    self.hT[:, 4 * h : 4 * h + 4, t * P : (t + 1) * P],
                    self.TR[:, t % 2, 512 * h : 512 * h + 512].rearrange("p (c q) -> p c q", c=4),
                ).then_inc(self.hT_ready, 1)

    def vector(self, nc, dve, st):
        dve.wait_ge(self.mod_in, 16 * 5)
        for s in range(2):
            st.did(
                nc.vector.scalar_tensor_tensor(
                    out=self.A[:, s, :], in0=self.A[:, s, :], scalar=1.0, in1=self.gain, op0=ALU.add, op1=ALU.mult
                )
            )
        dve.wait_ge(self.std_ready, 1)
        st.then(nc.vector.reciprocal(self.rstd[:], self.std[:]))
        for t in range(NT):
            s = stream(t)
            h = self.hN[:, t % 2, :]
            if t >= 2:
                dve.wait_ge(self.tr_ready, t - 1)
            st.then(
                nc.vector.scalar_tensor_tensor(
                    out=h, in0=self.X[:, t, :], scalar=self.rstd[:, t : t + 1], in1=self.A[:, s, :],
                    op0=ALU.mult, op1=ALU.mult,
                )
            )
            nc.vector.tensor_tensor(h, h, self.B[:, s, :], ALU.add).then_inc(self.h_ready, 1)

    def tensor(self, nc, pe, tiles=range(NT)):
        for t in tiles:
            pe.wait_ge(self.h_ready, t + 1)
            if t >= 2:
                pe.wait_ge(self.hT_ready, 2 * (t - 1))
            for c in range(DC):
                ins = nc.tensor.transpose(
                    self.TR[:, t % 2, c * P : (c + 1) * P], self.hN[:, t % 2, c * P : (c + 1) * P], self.ident[:]
                )
            ins.then_inc(self.tr_ready, 1)




def mixer_ab_stage(nc, io, mod_dram, X, x_in, ident, ones, eps):
    SC = float(HD) ** -0.5
    HT = TOK // 2
    with ExitStack() as ctx:
        m = Pool(nc, ctx, "ab")
        normbc = m.sb("normbc", [P, 5 * D])
        qk = normbc[:, 0 : NQK * TOK].rearrange("p (j t) -> p j t", j=NQK)
        hN = m.sb("hN", [P, 2, D])
        hT = m.sb("hT", [P, DC, TOK])
        yA = hT[:, 0:NQ, :]
        attn = hT[:, NQ:DC, :]
        prob = [attn[:, i, :] for i in range(2)]
        probT = [attn[:, 2 + i, :].rearrange("p (k q) -> p k q", q=P) for i in range(2)]
        WA = m.sb("WA", [P, DC, D])
        WB = m.sb("WB", [P, DC, D])
        uT = m.sb("uT", [P, GROUPS, TOK])
        vv = m.sb("vv", [P, NT, AW])
        vS = m.sb("vS", [P, NT, NKV * HD])
        g1 = m.sb("g1", [P, 2, D])
        sq = m.sb("sq", [P, 2, HT])
        qraw = m.sb("qraw", [P, 2, HT])
        stdq = m.sb("stdq", [P, 2, HT])
        qn = m.sb("qn", [P, 2, HT])
        t12 = m.sb("t12", [P, 2, HT])
        tmp = t12[:, :, :].rearrange("p a b -> p (a b)")[:, 0:512]
        cos, sin = m.sb("cos", [P, TOK]), m.sb("sin", [P, TOK])
        rotm = m.sb("rotm", [P, P])
        wsT = m.sb("wsT", [P, GROUPS, P])
        bsb = m.sb("bsb", [P, GROUPS, P])
        gcol = m.sb("gcol", [P, GROUPS])
        qkg = m.sb("qkg", [P, 2])
        ssv, stdv, rv = m.sb("ssv", [P, NT * GROUPS]), m.sb("stdv", [P, NT * GROUPS]), m.sb("rv", [P, NT * GROUPS])
        mx, nm = m.sb("mx", [P, 2]), m.sb("nm", [P, 2])
        psum_p, rp = m.sb("psum_p", [P, 2]), m.sb("rp", [P, 2])
        TR = m.ps("TR", [P, 2, D])
        MM = m.ps("MM", [P, 4, 512])

        norm = NormTranspose(m, X, ident, uT[:, 0:2, :].rearrange("p a b -> p (a b)")[:, 0:D], normbc, hT, hN, TR)
        norm.eps = eps
        wa_in, wb_in, wout_in, const_in, g1_in = (m.sem(x) for x in ("wa_in", "wb_in", "wout_in", "const_in", "g1_in"))
        mm_ready, mm_free = m.sem("mm_ready"), m.sem("mm_free")
        ssq_ready, stdq_ready, qn_ready, rot_ready, qk_done = (
            m.sem(x) for x in ("ssq_ready", "stdq_ready", "qn_ready", "rot_ready", "qk_done")
        )
        ssv_ready, stdv_ready, vvn_ready, gate_ready, gm_done = (
            m.sem(x) for x in ("ssv_ready", "stdv_ready", "vvn_ready", "gate_ready", "gm_done")
        )
        sc_ready, nm_ready, p_ready, pn_ready, ptr_ready, pt_ready, o_ready, o_done = (
            m.sem(x)
            for x in ("sc_ready", "nm_ready", "p_ready", "pn_ready", "ptr_ready", "pt_ready", "o_ready", "o_done")
        )
        y_ready, y_done, dve_step, act_step = m.sem("y_ready"), m.sem("y_done"), m.sem("dve_step"), m.sem("act_step")

        U0, V0, S0, Q0 = 0, 8, 8 + NT, 8 + 2 * NT
        QU = NQK * 2
        units = [(t, j) for t in range(NT) for j in range(NQ)]

        def nkeys(t):
            return CTX if t < CT else TOK

        with nc.Block() as block:

            @block.sync
            def _(sp):
                norm.load(nc, sp, io, mod_dram, 0)
                w = io["ab_w_in"][0].rearrange("(c p) n -> p c n", p=P)
                sp.dma_start(WA[:], w[:, :, 0:D]).then_inc(wa_in, 16)
                sp.dma_start(WB[:], w[:, :, D : 2 * D]).then_inc(wb_in, 16)
                bs_row = io["gmlp_bs"].rearrange("o g q -> (o g q)")
                for dst, src in (
                    (cos[:], io["cos"]), (sin[:], io["sin"]), (rotm[:], io["rotm"]), (wsT[:], io["wsT"]),
                    (bsb[:].rearrange("p g q -> p (g q)"), bs_row.partition_broadcast(P)),
                    (gcol[:], io["gmlp_gT"]), (qkg[:], io["qk_gT"]),
                ):
                    sp.dma_start(dst, src).then_inc(const_in, 16)
                for s in range(2):
                    sp.dma_start(g1[:, s, :], mod_dram[s, 0, 2].partition_broadcast(P)).then_inc(g1_in, 16)
                sp.wait_ge(mm_ready, S0)
                sp.dma_start(WA[:], io["ab_w_out"][0].rearrange("(c p) n -> p c n", p=P)).then_inc(wout_in, 16)

            @block.scalar
            def _(act):
                st = Steps(act, act_step)
                norm.scalar_sums(nc, act, lambda e, t: e.wait_ge(x_in[t], 16))
                for h in range(2):
                    norm.scalar_out(nc, act, range(h * NT // 2, (h + 1) * NT // 2))
                    for g in range(GROUPS):
                        n = U0 + GROUPS * h + g
                        act.wait_ge(mm_ready, n + 1)
                        nc.scalar.activation(
                            uT[:, g, h * HT : (h + 1) * HT], MM[:, n % 4, 0:HT], ACT.Gelu_apprx_tanh
                        ).then_inc(mm_free, 1)
                for t in range(NT):
                    n = V0 + t
                    act.wait_ge(mm_ready, n + 1)
                    nc.scalar.activation(vv[:, t, :], MM[:, n % 4, :], ACT.Gelu_apprx_tanh).then_inc(mm_free, 1)
                for t in range(NT):
                    n = S0 + t
                    act.wait_ge(mm_ready, n + 1)
                    nc.scalar.copy(vS[:, t, :], MM[:, n % 4, 0 : NKV * HD]).then_inc(mm_free, 1)
                act.wait_ge(ssv_ready, 1)
                nc.scalar.activation(stdv[:], ssv[:], ACT.Sqrt, bias=eps[:, 0:1], scale=1.0 / P).then_inc(stdv_ready, 1)
                act.wait_ge(const_in, 16 * 7)
                for u in range(QU + 1):
                    if u < QU:
                        n, par = Q0 + u, u % 2
                        act.wait_ge(mm_ready, n + 1)
                        if u >= 2:
                            act.wait_ge(ssq_ready, u - 1)
                            act.wait_ge(qn_ready, u - 1)
                        st.did(nc.scalar.square(sq[:, par, :], MM[:, n % 4, 0:HT]))
                        kind = 0 if u // 2 < NQ else 1
                        st.settle()
                        nc.scalar.activation(
                            qraw[:, par, :], MM[:, n % 4, 0:HT], ACT.Copy, scale=qkg[:, kind : kind + 1]
                        ).then_inc(mm_free, 1)
                    if u >= 1:
                        v, par = u - 1, (u - 1) % 2
                        act.wait_ge(ssq_ready, v + 1)
                        if v >= 2:
                            act.wait_ge(qn_ready, v - 1)
                        nc.scalar.activation(
                            stdq[:, par, :], TR[:, par, 0:HT], ACT.Sqrt, bias=eps[:, 0:1], scale=1.0 / HD
                        ).then_inc(stdq_ready, 1)
                for u in range(len(units) + 1):
                    if u < len(units):
                        t, j = units[u]
                        nk, par = nkeys(t), u % 2
                        act.wait_ge(nm_ready, u + 1)
                        if u >= 2:
                            act.wait_ge(ptr_ready, u - 1)
                        w = min(nk, HT)
                        nc.scalar.activation(
                            prob[par][:, 0:nk].rearrange("p (a k) -> p a k", k=w),
                            TR[:, par, :].rearrange("p (a k) -> p a k", a=2)[:, 0 : nk // w, 0:w],
                            ACT.Exp, bias=nm[:, par : par + 1], scale=SC, accum_out=psum_p[:, par : par + 1],
                        ).then_inc(p_ready, 1)
                    if u >= 1:
                        v = u - 1
                        nk, par = nkeys(units[v][0]), v % 2
                        act.wait_ge(ptr_ready, v + 1)
                        if v >= 2:
                            act.wait_ge(o_ready, v - 1)
                        k3 = min(nk // P, 3)
                        nc.scalar.copy(
                            probT[par][:, 0 : nk // P, :].rearrange("p (a k) q -> p a k q", k=k3),
                            MM[:, 0 : nk // P // k3, 0 : k3 * P].rearrange("p a (k q) -> p a k q", q=P),
                        ).then_inc(pt_ready, 1)

            @block.vector
            def _(dve):
                st = Steps(dve, dve_step)
                norm.vector(nc, dve, st)
                for t in range(NT):
                    dve.wait_ge(mm_free, V0 + t + 1)
                    st.then(nc.vector.tensor_tensor(tmp, vv[:, t, :], vv[:, t, :], ALU.mult))
                    ins = nc.vector.reduce_sum(
                        ssv[:, GROUPS * t : GROUPS * (t + 1)], tmp.rearrange("p (g c) -> p g c", g=GROUPS), AX
                    )
                    st.then(ins)
                dve.sem_inc(ssv_ready, 1)
                dve.wait_ge(stdv_ready, 1)
                st.then(nc.vector.reciprocal(rv[:], stdv[:]))
                for t in range(NT):
                    v3 = vv[:, t, :].rearrange("p (g c) -> p g c", g=GROUPS)
                    nc.vector.tensor_tensor(
                        v3, v3, rv[:, GROUPS * t : GROUPS * (t + 1)].unsqueeze(2).to_broadcast([P, GROUPS, P]), ALU.mult
                    ).then_inc(vvn_ready, 1)
                dve.wait_ge(const_in, 16 * 7)
                for u in range(QU + 1):
                    if u < QU:
                        par = u % 2
                        dve.wait_ge(stdq_ready, u + 1)
                        st.then(nc.vector.reciprocal(stdq[:, par, :], stdq[:, par, :]))
                        dve.wait_ge(mm_free, Q0 + u + 1)
                        nc.vector.tensor_tensor(qn[:, par, :], qraw[:, par, :], stdq[:, par, :], ALU.mult).then_inc(
                            qn_ready, 1
                        )
                    if u >= 1:
                        v, par = u - 1, (u - 1) % 2
                        j, h = v // 2, v % 2
                        cols = slice(h * HT, (h + 1) * HT)
                        dve.wait_ge(rot_ready, v + 1)
                        dve.wait_ge(qn_ready, v + 1)
                        st.did(nc.vector.tensor_tensor(t12[:, 0, :], qn[:, par, :], cos[:, cols], ALU.mult))
                        st.then(nc.vector.tensor_tensor(t12[:, 1, :], TR[:, par, 512 : 512 + HT], sin[:, cols], ALU.mult))
                        nc.vector.tensor_tensor(qk[:, j, cols], t12[:, 0, :], t12[:, 1, :], ALU.add).then_inc(qk_done, 1)
                        dve.wait_ge(qk_done, v + 1)
                for t in range(NT):
                    dve.wait_ge(gate_ready, t + 1)
                    for g in range(GROUPS):
                        st.did(
                            nc.vector.scalar_tensor_tensor(
                                out=tmp[:, g * P : (g + 1) * P], in0=MM[:, t % 4, g * P : (g + 1) * P],
                                scalar=gcol[:, g : g + 1], in1=bsb[:, g, :], op0=ALU.mult, op1=ALU.add,
                            )
                        )
                    st.settle()
                    ut = uT[:, :, t * P : (t + 1) * P]
                    nc.vector.tensor_tensor(ut, ut, tmp.rearrange("p (g q) -> p g q", g=GROUPS), ALU.mult).then_inc(
                        gm_done, 1
                    )
                    dve.wait_ge(gm_done, t + 1)
                for u in range(len(units) + 2):
                    if 1 <= u <= len(units):
                        v, par = u - 1, (u - 1) % 2
                        nk = nkeys(units[v][0])
                        dve.wait_ge(p_ready, v + 1)
                        st.then(nc.vector.reciprocal(rp[:, par : par + 1], psum_p[:, par : par + 1]))
                        nc.vector.tensor_scalar(
                            prob[par][:, 0:nk], prob[par][:, 0:nk], rp[:, par : par + 1], None, ALU.mult
                        ).then_inc(pn_ready, 1)
                    if u < len(units):
                        t, j = units[u]
                        nk, par = nkeys(t), u % 2
                        w = min(nk, HT)
                        dve.wait_ge(sc_ready, u + 1)
                        if u >= 2:
                            dve.wait_ge(p_ready, u - 1)
                        st.then(
                            nc.vector.tensor_reduce(
                                mx[:, par : par + 1],
                                TR[:, par, :].rearrange("p (a k) -> p a k", a=2)[:, 0 : nk // w, 0:w],
                                mybir.AxisListType.XY, ALU.max,
                            )
                        )
                        nc.vector.tensor_scalar(nm[:, par : par + 1], mx[:, par : par + 1], -SC, None, ALU.mult).then_inc(
                            nm_ready, 1
                        )
                    if u >= 2:
                        v, par = u - 2, u % 2
                        t, j = units[v]
                        dve.wait_ge(o_ready, v + 1)
                        nc.vector.tensor_copy(yA[:, j, t * P : (t + 1) * P], MM[:, 2 + par, 0:P]).then_inc(o_done, 1)
                dve.wait_ge(g1_in, 32)
                for n in range(2 * NT):
                    t, h = n // 2, n % 2
                    cols = slice(512 * h, 512 * h + 512)
                    dve.wait_ge(y_ready, n + 1)
                    if n:
                        dve.wait_ge(y_done, n)
                    st.then(
                        nc.vector.tensor_tensor(
                            tmp, TR[:, n % 4 // 2, 512 * (n % 2) : 512 * (n % 2) + 512], g1[:, stream(t), cols], ALU.mult
                        )
                    )
                    nc.vector.tensor_tensor(X[:, t, cols], X[:, t, cols], tmp, ALU.add).then_inc(y_done, 1)

            @block.tensor
            def _(pe):
                def bank(n):
                    if n >= 4:
                        pe.wait_ge(mm_free, n - 3)
                    return MM[:, n % 4, :]

                def project_cols(n, W, c0, h):
                    out = bank(n)[:, 0:HT]
                    for c in range(DC):
                        ins = nc.tensor.matmul(
                            out, W[:, c, c0 : c0 + P], hT[:, c, h * HT : (h + 1) * HT], start=(c == 0), stop=(c == DC - 1)
                        )
                    ins.then_inc(mm_ready, 1)

                def project_rows(n, W, c0, width, t):
                    out = bank(n)[:, 0:width]
                    for c in range(DC):
                        ins = nc.tensor.matmul(
                            out, hT[:, c, t * P : (t + 1) * P], W[:, c, c0 : c0 + width], start=(c == 0), stop=(c == DC - 1)
                        )
                    ins.then_inc(mm_ready, 1)

                for h in range(2):
                    norm.tensor(nc, pe, range(h * NT // 2, (h + 1) * NT // 2))
                    pe.wait_ge(norm.hT_ready, (h + 1) * NT)
                    pe.wait_ge(wa_in, 16)
                    for g in range(GROUPS):
                        project_cols(U0 + GROUPS * h + g, WA, g * P, h)
                for t in range(NT):
                    project_rows(V0 + t, WA, AW, AW, t)
                pe.wait_ge(wb_in, 16)
                for t in range(NT):
                    project_rows(S0 + t, WB, NQK * HD, NKV * HD, t)
                pe.wait_ge(const_in, 16 * 7)
                for u in range(QU + 2):
                    if u < QU:
                        project_cols(Q0 + u, WB, (u // 2) * HD, u % 2)
                    if 1 <= u <= QU:
                        v, par = u - 1, (u - 1) % 2
                        pe.wait_ge(mm_free, Q0 + v + 1)
                        if v >= 2:
                            pe.wait_ge(stdq_ready, v - 1)
                        nc.tensor.matmul(TR[:, par, 0:HT], ones[:], sq[:, par, :], start=True, stop=True).then_inc(
                            ssq_ready, 1
                        )
                    if u >= 2:
                        v, par = u - 2, u % 2
                        pe.wait_ge(qn_ready, v + 1)
                        if v >= 2:
                            pe.wait_ge(qk_done, v - 1)
                        nc.tensor.matmul(
                            TR[:, par, 512 : 512 + HT], rotm[:], qn[:, par, :], start=True, stop=True
                        ).then_inc(rot_ready, 1)
                pe.wait_ge(mm_free, Q0 + QU)
                for t in range(NT):
                    pe.wait_ge(vvn_ready, t + 1)
                    if t >= 4:
                        pe.wait_ge(gm_done, t - 3)
                    for g in range(GROUPS):
                        ins = nc.tensor.matmul(
                            MM[:, t % 4, g * P : (g + 1) * P], vv[:, t, g * P : (g + 1) * P], wsT[:, g, :],
                            start=True, stop=True,
                        )
                    ins.then_inc(gate_ready, 1)

                def scores(u):
                    t, j = units[u]
                    nk, par = nkeys(t), u % 2
                    w = min(nk, HT)
                    if u >= 2:
                        pe.wait_ge(p_ready, u - 1)
                    for a in range(nk // w):
                        ins = nc.tensor.matmul(
                            TR[:, par, 512 * a : 512 * a + w], qk[:, j, t * P : (t + 1) * P],
                            qk[:, NQ + j // (NQ // NKV), a * w : (a + 1) * w], start=True, stop=True,
                        )
                    ins.then_inc(sc_ready, 1)

                def turn(u):
                    nk, par = nkeys(units[u][0]), u % 2
                    pe.wait_ge(pn_ready, u + 1)
                    if u >= 1:
                        pe.wait_ge(pt_ready, u)
                    k3 = min(nk // P, 3)
                    for k in range(nk // P):
                        ins = nc.tensor.transpose(
                            MM[:, k // k3, (k % k3) * P : (k % k3 + 1) * P], prob[par][:, k * P : (k + 1) * P], ident[:]
                        )
                    ins.then_inc(ptr_ready, 1)

                def weigh(u):
                    t, j = units[u]
                    nk, par = nkeys(t), u % 2
                    kv = j // (NQ // NKV)
                    pe.wait_ge(pt_ready, u + 1)
                    if u >= 2:
                        pe.wait_ge(o_done, u - 1)
                    for k in range(nk // P):
                        ins = nc.tensor.matmul(
                            MM[:, 2 + par, 0:P], vS[:, k, kv * HD : (kv + 1) * HD], probT[par][:, k, :],
                            start=(k == 0), stop=(k == nk // P - 1),
                        )
                    ins.then_inc(o_ready, 1)

                pe.wait_ge(qk_done, QU)
                pe.wait_ge(gm_done, NT)
                for u in range(-1, len(units) + 1):
                    if u + 1 < len(units):
                        scores(u + 1)
                    if 0 <= u < len(units):
                        turn(u)
                    if u >= 1:
                        weigh(u - 1)
                pe.wait_ge(o_done, len(units))
                pe.wait_ge(wout_in, 16)
                pe.wait_ge(p_ready, len(units))
                for n in range(2 * NT):
                    t, h = n // 2, n % 2
                    if n >= 4:
                        pe.wait_ge(y_done, n - 3)
                    out = TR[:, n % 4 // 2, 512 * (n % 2) : 512 * (n % 2) + 512]
                    for k in range(DC):
                        src = uT[:, k, :] if k < GROUPS else yA[:, k - GROUPS, :]
                        ins = nc.tensor.matmul(
                            out, src[:, t * P : (t + 1) * P], WA[:, k, 512 * h : 512 * h + 512],
                            start=(k == 0), stop=(k == DC - 1),
                        )
                    ins.then_inc(y_ready, 1)




def peer_stage(nc, io, mod_dram, X, ident, eps, layer, T0, out):
    M = NT - T0
    RING = 4
    AHEAD = 1
    STREAMS = sorted({stream(t) for t in range(T0, NT)})
    u_tab, v_tab = io[f"peer_u{layer}"], io[f"peer_v{layer}"]
    with ExitStack() as ctx:
        m = Pool(nc, ctx, f"peer{layer}")
        wq = m.sb("wq", [P, DC, 2 * HEADS * KEYS])
        keys = m.sb("keys", [P, 2 * HEADS, KEYS])
        A, B, g2 = m.sb("A", [P, 2, D]), m.sb("B", [P, 2, D]), m.sb("g2", [P, 2, D])
        gain = m.sb("gain", [P, D])
        iota = m.sb("iota", [P, TOPK])
        U, V = m.sb("U", [P, RING, D]), m.sb("V", [P, RING, D])
        h_next, h_cur = m.sb("h_next", [P, D]), m.sb("h_cur", [P, D])
        hT = m.sb("hT", [P, DC, P])
        qT = m.sb("qT", [P, 2, 2, P])
        diag = m.sb("diag", [P, RING, P])
        h_tmp = m.sb("h_tmp", [P, D])
        ss, rstd = m.sb("ss", [P, M]), m.sb("rstd", [P, M])
        S, S2 = m.sb("S", [P, 2, KEYS]), m.sb("S2", [P, 2, KEYS])
        best, ibest = m.sb("best", [P, 2, TOPK]), m.sb("ibest", [P, 2, TOPK], U32)
        cand, cand2 = m.sb("cand", [P, TOPK, TOPK]), m.sb("cand2", [P, TOPK, TOPK])
        top, pos = m.sb("top", [P, TOPK]), m.sb("pos", [P, TOPK], U32)
        half_pos = m.sb("half_pos", [P, 2, TOPK], U32)
        hot = m.sb("hot", [P, 2, TOPK, TOPK])
        half_idx = m.sb("half_idx", [P, 2, TOPK])
        experts = m.sb("experts", [P, SLOTS], U32)
        zero = m.sb("zero", [P, 1], U32)
        GATES = 4
        gate, gsum = m.sb("gate", [P, GATES, TOPK]), m.sb("gsum", [P, GATES])
        fin = m.sb("fin", [P, 3 * M])
        idx = m.sb("idx", [P, 2, TOPK], U32)
        dots, act_out, wgt = m.sb("dots", [P, 2, TOPK]), m.sb("act_out", [P, 2, TOPK]), m.sb("wgt", [P, 2, TOPK])
        psT = m.ps("psT", [P, D])
        psq = m.ps("psq", [P, 2, 512])
        psS = m.ps("psS", [P, 2, 512])
        psY = m.ps("psY", [P, D])

        const_in = m.sem("const_in")
        keys_in = m.sem("keys_in")
        wq_parts = ((0, 1), (1, AHEAD + 1), (AHEAD + 1, HEADS))
        wq_in = [m.sem(f"wq_in{i}") for i in range(3)]
        sq_done, std_ready, h_ready, tr_ready, hT_ready = (
            m.sem(x) for x in ("sq_done", "std_ready", "h_ready", "tr_ready", "hT_ready")
        )
        q_ready, q_copied, s_ready, chosen = (m.sem(x) for x in ("q_ready", "q_copied", "s_ready", "chosen"))
        g_exp = m.sem("g_exp")
        u_in = [m.sem(f"u_in{r}") for r in range(RING)]
        v_in = [m.sem(f"v_in{r}") for r in range(RING)]
        u_used, v_used = m.sem("u_used"), m.sem("v_used")
        act_ready, w_ready, diag_ready, y_ready, y_taken, idx_copied, dve_step, x_done = (
            m.sem(x)
            for x in ("act_ready", "w_ready", "diag_ready", "y_ready", "y_taken", "idx_copied", "dve_step", "x_done")
        )
        zero_set, g2_in = m.sem("zero_set"), m.sem("g2_in")
        gain_free, gain_in = m.sem("gain_free"), m.sem("gain_in")
        fin_sq, fin_std, fin_done, stored = (m.sem(x) for x in ("fin_sq", "fin_std", "fin_done", "stored"))

        def turns(eng, turn):
            turn(0)
            with eng.Fori(1, M - 1) as j:
                turn(j)
            turn(M - 1)

        def first(j):
            return isinstance(j, int) and j == 0

        def heads_from(j, hd):
            return HEADS - 1 - hd if isinstance(j, int) and j == M - 1 else HEADS

        with nc.Block() as block:

            @block.sync
            def _(sp):
                w = io["peer_wq"][layer].rearrange("(c p) n -> p c n", p=P)
                sp.dma_start(gain[:], io["norm2_g"][layer].partition_broadcast(P)).then_inc(const_in, 16)
                for s in STREAMS:
                    for dst, k in ((A, 4), (B, 3)):
                        sp.dma_start(dst[:, s, :], mod_dram[s, layer, k].partition_broadcast(P)).then_inc(const_in, 16)

                def load_wq(i):
                    cols = slice(2 * KEYS * wq_parts[i][0], 2 * KEYS * wq_parts[i][1])
                    sp.dma_start(wq[:, :, cols], w[:, :, cols]).then_inc(wq_in[i], 16)

                load_wq(0)
                sp.dma_start(keys[:], io["keysT"][layer]).then_inc(keys_in, 16)
                sp.dma_start(iota[:], io["iota"]).then_inc(keys_in, 16)
                load_wq(1)
                load_wq(2)
                for s in STREAMS:
                    sp.dma_start(g2[:, s, :], mod_dram[s, layer, 5].partition_broadcast(P)).then_inc(g2_in, 16)
                if out is not None:
                    o = out.rearrange("o (t p) d -> p (o t) d", p=P)
                    sp.wait_ge(gain_free, 1)
                    sp.dma_start(gain[:], io["final_norm_g"].partition_broadcast(P)).then_inc(gain_in, 16)
                    for t in range(M):
                        sp.wait_ge(fin_done, t + 1)
                        sp.dma_start(o[:, t, :], X[:, T0 + t, :]).then_inc(stored, 16)
                    sp.wait_ge(stored, 16 * M)

            @block.gpsimd
            def _(pool):
                def take(n_par, hd, k):
                    src = experts[:, hd * TOPK + k : hd * TOPK + k + 1]
                    pool.tensor_tensor(idx[:, n_par, k : k + 1], src, zero[:], ALU.add).then_inc(idx_copied, 1)

                def rows(table, ring, n_par, k, arrived):
                    pool.indirect_dma_start(
                        ring[:, k % RING, :], None, table, bass.IndirectOffsetOnAxis(ap=idx[:, n_par, k : k + 1], axis=0)
                    ).then_inc(arrived[k % RING], 16)

                pool.memset(zero[:], 0).then_inc(zero_set, 1)
                pool.wait_ge(zero_set, 1)
                pool.wait_ge(chosen, 1)
                take(0, 0, 0)
                for k in range(TOPK):
                    if k < TOPK - 1:
                        take(0, 0, k + 1)
                    pool.wait_ge(idx_copied, k + 1)
                    pool.wait_ge(u_used, k + 1)
                    rows(u_tab, U, 0, k, u_in)
                pool.wait_ge(chosen, 2)
                take(1, 1, 0)

                def head(j, hd, heads_left):
                    n, par = j * HEADS + hd, hd % 2
                    for k in range(TOPK):
                        pool.wait_ge(v_used, n * TOPK + (k + 1))
                        if heads_left >= 1:
                            pool.wait_ge(u_used, n * TOPK + (TOPK + k + 1))
                            pool.wait_ge(idx_copied, n * TOPK + (TOPK + k + 1))
                            if k < TOPK - 1:
                                take(1 - par, (hd + 1) % HEADS, k + 1)
                            elif heads_left >= 2:
                                pool.wait_ge(chosen, n + 3)
                                take(par, (hd + 2) % HEADS, 0)
                        rows(v_tab, V, par, k, v_in)
                        if heads_left >= 1:
                            rows(u_tab, U, 1 - par, k, u_in)

                def turn(j):
                    for hd in range(HEADS):
                        head(j, hd, heads_from(j, hd))

                turns(pool, turn)

            @block.scalar
            def _(act):
                for t in range(M):
                    nc.scalar.activation(
                        V[:, t % RING, :], X[:, T0 + t, :], ACT.Square, accum_out=ss[:, t : t + 1]
                    ).then_inc(sq_done, 1)
                    if t < M - 1 and t % RING == RING - 1:
                        act.wait_ge(sq_done, t + 1)
                act.wait_ge(sq_done, M)
                nc.scalar.activation(rstd[:], ss[:], ACT.Sqrt, bias=eps[:, 0:1], scale=1.0 / D).then_inc(std_ready, 1)

                def copy_hT(t):
                    act.wait_ge(tr_ready, t + 1)
                    for h in range(2):
                        nc.scalar.copy(
                            hT[:, 4 * h : 4 * h + 4, :],
                            psT[:, 512 * h : 512 * h + 512].rearrange("p (c q) -> p c q", c=4),
                        ).then_inc(hT_ready, 1)

                def copy_query(w, par):
                    act.wait_ge(q_ready, w + 1)
                    if not (isinstance(w, int) and w < 2):
                        act.wait_ge(s_ready, w - 1)
                    nc.scalar.copy(
                        qT[:, par, :, :], psq[:, par, 0 : 2 * P].rearrange("p (s q) -> p s q", s=2)
                    ).then_inc(q_copied, 1)

                copy_hT(0)
                for w in range(AHEAD + 1):
                    copy_query(w, w % 2)

                def turn(j):
                    for hd in range(HEADS):
                        n, par, gp = j * HEADS + hd, hd % 2, hd % GATES
                        act.wait_ge(chosen, n + 1)
                        nc.scalar.activation(
                            gate[:, gp, :], gate[:, gp, :], ACT.Exp, accum_out=gsum[:, gp : gp + 1]
                        ).then_inc(g_exp, 1)
                        act.wait_ge(u_used, n * TOPK + (RING + TOPK))
                        if not (first(j) and hd < 2):
                            act.wait_ge(w_ready, n - 1)
                        nc.scalar.activation(act_out[:, par, :], dots[:, par, :], ACT.Gelu_apprx_tanh).then_inc(
                            act_ready, 1
                        )
                        if heads_from(j, hd) > AHEAD:
                            if hd + AHEAD + 1 == HEADS:
                                copy_hT(j + 1)
                            copy_query(n + (AHEAD + 1), (hd + AHEAD + 1) % 2)
                        act.wait_ge(w_ready, n + 1)
                        for k in range(TOPK):
                            act.wait_ge(v_used, n * TOPK + (k + 1))
                            nc.scalar.activation(
                                diag[:, k % RING, :], ident[:], ACT.Copy, scale=wgt[:, par, k : k + 1]
                            ).then_inc(diag_ready, 1)

                turns(act, turn)
                if out is not None:
                    for t in range(M):
                        act.wait_ge(x_done, 2 * t + 2)
                        if t >= 2:
                            act.wait_ge(fin_sq, t - 1)
                        nc.scalar.activation(
                            U[:, t % 2, :], X[:, T0 + t, :], ACT.Square, accum_out=fin[:, t : t + 1]
                        ).then_inc(fin_sq, 1)
                    act.wait_ge(fin_sq, M)
                    nc.scalar.activation(
                        fin[:, M : 2 * M], fin[:, 0:M], ACT.Sqrt, bias=eps[:, 0:1], scale=1.0 / D
                    ).then_inc(fin_std, 1)

            @block.vector
            def _(dve):
                st = Steps(dve, dve_step)
                dve.sem_inc(u_used, RING)
                dve.wait_ge(const_in, 16 * (1 + 2 * len(STREAMS)))
                for s in STREAMS:
                    st.did(
                        nc.vector.scalar_tensor_tensor(
                            out=A[:, s, :], in0=A[:, s, :], scalar=1.0, in1=gain[:], op0=ALU.add, op1=ALU.mult
                        )
                    )
                dve.wait_ge(std_ready, 1)
                st.did(nc.vector.reciprocal(rstd[:], rstd[:]))
                st.restart()
                if out is not None:
                    dve.sem_inc(gain_free, 1)

                def normalise(c):
                    x = X[:, bass.ds(c + T0, 1), :].rearrange("p o d -> p (o d)")
                    s = stream(c + T0)
                    a = A[:, bass.ds(s, 1), :].rearrange("p o d -> p (o d)")
                    b = B[:, bass.ds(s, 1), :].rearrange("p o d -> p (o d)")
                    st.then(
                        nc.vector.scalar_tensor_tensor(
                            out=h_next[:], in0=x, scalar=rstd[:, bass.ds(c, 1)], in1=a, op0=ALU.mult, op1=ALU.mult
                        )
                    )
                    st.then(nc.vector.tensor_tensor(h_next[:], h_next[:], b, ALU.add))
                    st.restart()
                    dve.sem_inc(h_ready, 1)


                def best8_of_halves(w, par):
                    dve.wait_ge(s_ready, w + 1)
                    if not (isinstance(w, int) and w == 0):
                        dve.wait_ge(chosen, w)
                    else:
                        dve.wait_ge(keys_in, 32)
                    st.then(nc.vector.tensor_copy(S[:], psS[:, par, 0 : 2 * KEYS].rearrange("p (s k) -> p s k", s=2)))
                    for s in range(2):
                        st.did(nc.vector.max(best[:, s, 0:8], S[:, s, :]))

                def drop_best8():
                    st.settle()
                    for s in range(2):
                        st.did(nc.vector.max_index(ibest[:, s, 0:8], best[:, s, 0:8], S[:, s, :]))
                        st.did(nc.vector.match_replace(S2[:, s, :], best[:, s, 0:8], S[:, s, :], BIG))

                def next8_of_halves():
                    st.settle()
                    for s in range(2):
                        st.did(nc.vector.max(best[:, s, 8:16], S2[:, s, :]))
                    st.settle()
                    for s in range(2):
                        st.did(nc.vector.max_index(ibest[:, s, 8:16], best[:, s, 8:16], S2[:, s, :]))

                c1, c2 = cand[:].rearrange("p a b -> p (a b)"), cand2[:].rearrange("p a b -> p (a b)")

                def best8_of_sums():
                    st.settle()
                    st.then(
                        nc.vector.tensor_tensor(
                            cand[:], best[:, 0, :].unsqueeze(2).to_broadcast([P, TOPK, TOPK]),
                            best[:, 1, :].unsqueeze(1).to_broadcast([P, TOPK, TOPK]), ALU.add,
                        )
                    )
                    st.then(nc.vector.max(top[:, 0:8], c1))
                    st.did(nc.vector.max_index(pos[:, 0:8], top[:, 0:8], c1))
                    st.did(nc.vector.match_replace(c2, top[:, 0:8], c1, BIG))

                def next8_of_sums():
                    st.settle()
                    st.then(nc.vector.max(top[:, 8:16], c2))
                    st.then(nc.vector.max_index(pos[:, 8:16], top[:, 8:16], c2))
                    st.did(nc.vector.tensor_scalar(half_pos[:, 0, :], pos[:], 4, None, ALU.logical_shift_right))
                    st.did(nc.vector.tensor_scalar(half_pos[:, 1, :], pos[:], TOPK - 1, None, ALU.bitwise_and))

                def positions_to_experts(w, hd, tile_0):
                    st.settle()
                    for s in range(2):
                        st.did(
                            nc.vector.tensor_tensor(
                                hot[:, s, :, :], half_pos[:, s, :].unsqueeze(2).to_broadcast([P, TOPK, TOPK]),
                                iota[:].unsqueeze(1).to_broadcast([P, TOPK, TOPK]), ALU.is_equal,
                            )
                        )
                    st.settle()
                    for s in range(2):
                        st.did(
                            nc.vector.tensor_tensor(
                                hot[:, s, :, :], hot[:, s, :, :],
                                ibest[:, s, :].unsqueeze(1).to_broadcast([P, TOPK, TOPK]), ALU.mult,
                            )
                        )
                    st.settle()
                    for s in range(2):
                        st.did(nc.vector.reduce_sum(half_idx[:, s, :], hot[:, s, :, :], AX))
                    st.then(nc.vector.tensor_scalar(gate[:, hd % GATES, :], top[:], top[:, 0:1], None, ALU.subtract))
                    st.restart()
                    if not tile_0:
                        dve.wait_ge(idx_copied, (w - HEADS) * TOPK + TOPK)
                    nc.vector.scalar_tensor_tensor(
                        out=experts[:, hd * TOPK : (hd + 1) * TOPK], in0=half_idx[:, 0, :], scalar=float(KEYS), in1=half_idx[:, 1, :],
                        op0=ALU.mult, op1=ALU.add,
                    ).then_inc(chosen, 1)

                def choice_step(step, w, hd, tile_0):
                    if step == 0:
                        best8_of_halves(w, hd % 2)
                    elif step == 1:
                        drop_best8()
                    elif step == 2:
                        next8_of_halves()
                    elif step == 3:
                        best8_of_sums()
                    elif step == 4:
                        next8_of_sums()
                    else:
                        positions_to_experts(w, hd, tile_0)

                def add_tile(j):
                    t = j + T0
                    g = g2[:, bass.ds(stream(t), 1), :].rearrange("p o d -> p (o d)")
                    x = X[:, bass.ds(t, 1), :].rearrange("p o d -> p (o d)")
                    for h in range(2):
                        cols = slice(512 * h, 512 * h + 512)
                        dve.wait_ge(y_ready, j + 1)
                        if h:
                            dve.wait_ge(x_done, j * 2 + 1)
                        st.then(nc.vector.tensor_tensor(h_tmp[:, cols], psY[:, cols], g[:, cols], ALU.mult))
                        st.restart()
                        nc.vector.tensor_tensor(x[:, cols], x[:, cols], h_tmp[:, cols], ALU.add).then_inc(x_done, 1)
                    dve.sem_inc(y_taken, 1)

                normalise(0)
                for w in range(AHEAD):
                    for step in range(6):
                        choice_step(step, w, w, True)

                def turn(j):
                    st.then(nc.vector.tensor_copy(h_cur[:], h_next[:]))
                    st.restart()
                    for hd in range(HEADS):
                        n, par, gp = j * HEADS + hd, hd % 2, hd % GATES
                        choosing = heads_from(j, hd) >= AHEAD
                        if not (first(j) and hd < 2):
                            dve.wait_ge(act_ready, n - 1)
                        for k in range(TOPK):
                            r = k % RING
                            dve.wait_ge(u_in[r], n * (16 * TOPK // RING) + 16 * (k // RING + 1))
                            nc.vector.tensor_tensor_reduce(
                                U[:, r, :], U[:, r, :], h_cur[:], 1.0, 0.0, ALU.mult, ALU.add,
                                dots[:, par, k : k + 1],
                            ).then_inc(u_used, 1)
                            if choosing and k % 2 == 1 and k < 12:
                                tile_0 = first(j) and hd + AHEAD < HEADS
                                choice_step(k // 2, n + AHEAD, (hd + AHEAD) % HEADS, tile_0)
                        if hd == 0 and not first(j):
                            add_tile(j - 1)
                        dve.wait_ge(g_exp, n + 1)
                        st.did(nc.vector.reciprocal(gsum[:, gp : gp + 1], gsum[:, gp : gp + 1]))
                        st.restart()
                        dve.wait_ge(act_ready, n + 1)
                        if not (first(j) and hd < 2):
                            dve.wait_ge(diag_ready, n * TOPK - TOPK)
                        nc.vector.scalar_tensor_tensor(
                            out=wgt[:, par, :], in0=gate[:, gp, :], scalar=gsum[:, gp : gp + 1],
                            in1=act_out[:, par, :], op0=ALU.mult, op1=ALU.mult,
                        ).then_inc(w_ready, 1)
                        if hd + AHEAD + 2 == HEADS and heads_from(j, hd) == HEADS:
                            normalise(j + 1)

                dve.wait_ge(g2_in, 16 * len(STREAMS))
                turns(dve, turn)
                add_tile(M - 1)
                if out is not None:
                    dve.wait_ge(fin_std, 1)
                    dve.wait_ge(gain_in, 16)
                    st.then(nc.vector.reciprocal(fin[:, 2 * M : 3 * M], fin[:, M : 2 * M]))
                    for t in range(M):
                        nc.vector.scalar_tensor_tensor(
                            out=X[:, T0 + t, :], in0=X[:, T0 + t, :], scalar=fin[:, 2 * M + t : 2 * M + t + 1],
                            in1=gain[:], op0=ALU.mult, op1=ALU.mult,
                        ).then_inc(fin_done, 1)

            @block.tensor
            def _(pe):
                pe.sem_inc(v_used, RING)
                def transpose_h(t):
                    pe.wait_ge(h_ready, t + 1)
                    for k in range(DC):
                        ins = nc.tensor.transpose(psT[:, k * P : (k + 1) * P], h_next[:, k * P : (k + 1) * P], ident[:])
                    ins.then_inc(tr_ready, 1)
                    pe.wait_ge(hT_ready, t * 2 + 2)

                def score_head(w, hd):
                    par = hd % 2
                    if not (isinstance(w, int) and w < 2):
                        pe.wait_ge(q_copied, w - 1)
                    for s in range(2):
                        c0 = (2 * hd + s) * P
                        for k in range(DC):
                            ins = nc.tensor.matmul(
                                psq[:, par, s * P : (s + 1) * P], wq[:, k, c0 : c0 + P], hT[:, k, :],
                                start=(k == 0), stop=(k == DC - 1),
                            )
                    ins.then_inc(q_ready, 1)
                    pe.wait_ge(q_copied, w + 1)
                    if not (isinstance(w, int) and w < 2):
                        pe.wait_ge(chosen, w - 1)
                    for s in range(2):
                        ins = nc.tensor.matmul(
                            psS[:, par, s * KEYS : (s + 1) * KEYS], qT[:, par, s, :], keys[:, 2 * hd + s, :],
                            start=True, stop=True,
                        )
                    ins.then_inc(s_ready, 1)

                transpose_h(0)
                pe.wait_ge(wq_in[0], 16)
                pe.wait_ge(keys_in, 32)
                score_head(0, 0)
                pe.wait_ge(wq_in[1], 16)
                for w in range(1, AHEAD + 1):
                    score_head(w, w)
                pe.wait_ge(wq_in[2], 16)

                def turn(j):
                    for hd in range(HEADS):
                        n = j * HEADS + hd
                        if heads_from(j, hd) > AHEAD:
                            if hd + AHEAD + 1 == HEADS:
                                transpose_h(j + 1)
                            score_head(n + (AHEAD + 1), (hd + AHEAD + 1) % HEADS)
                        if hd == 0 and not first(j):
                            pe.wait_ge(y_taken, j)
                        for k in range(TOPK):
                            r = k % RING
                            pe.wait_ge(diag_ready, n * TOPK + (k + 1))
                            pe.wait_ge(v_in[r], n * (16 * TOPK // RING) + 16 * (k // RING + 1))
                            for h in range(2):
                                cols = slice(512 * h, 512 * h + 512)
                                ins = nc.tensor.matmul(
                                    psY[:, cols], diag[:, r, :], V[:, r, cols],
                                    start=(hd == 0 and k == 0), stop=(hd == HEADS - 1 and k == TOPK - 1),
                                )
                            ins.then_inc(v_used, 1)
                        if hd == HEADS - 1:
                            pe.wait_ge(v_used, n * TOPK + (RING + TOPK))
                            pe.sem_inc(y_ready, 1)

                turns(pe, turn)




def mixer_rg_stage(nc, io, mod_dram, X, ident, eps):
    with ExitStack() as outer:
        mo = Pool(nc, outer, "rg")
        XC = mo.sb("XC", [P, RB, XCW])
        G = mo.sb("G", [P, RB, SEQ])
        wg = mo.sb("wg", [P, 4, RB, P])
        g1 = mo.sb("g1", [P, D])
        hT = mo.sb("hT", [P, DC, TOK])
        cl, cl2 = mo.sb("cl", [P, 2, RB]), mo.sb("cl2", [P, 2, RB])
        ba, bx = mo.sb("ba", [P, 2, RB]), mo.sb("bx", [P, 2, RB])
        rg_input_part(nc, io, mod_dram, X, ident, eps, hT, XC, G, wg, g1, cl, cl2, ba, bx)
        rg_scan_part(nc, io, X, hT, XC, G, wg, g1, cl, cl2, ba, bx)


def rg_input_part(nc, io, mod_dram, X, ident, eps, hT, XC, G, wg, g1, cl, cl2, ba, bx):
    RING = 6
    with ExitStack() as ctx:
        m = Pool(nc, ctx, "rgi")
        normbc = m.sb("normbc", [P, 5 * D])
        hN = m.sb("hN", [P, 2, D])
        W = m.sb("W", [P, RING, DC, P])
        raw = m.sb("raw", [P, 2, RAWW])
        cw, cb = m.sb("cw", [P, RB, CONV]), m.sb("cb", [P, RB])
        lam = m.sb("lam", [P, 2, RB])
        e1, z, z2, poly = (m.sb(x, [P, 2, RB]) for x in ("e1", "z", "z2", "poly"))
        TR = m.ps("TR", [P, 2, D])
        MM = m.ps("MM", [P, 4, 512])
        norm = NormTranspose(m, X, ident, G[:, 0:2, :].rearrange("p a b -> p (a b)"), normbc, hT, hN, TR)
        norm.eps = eps
        w_in = [m.sem(f"w_in{r}") for r in range(RING)]
        small_in, late_in = m.sem("small_in"), m.sem("late_in")
        mm_ready, mm_free, conv_done, dve_step, e_ready = (
            m.sem(x) for x in ("mm_ready", "mm_free", "conv_done", "dve_step", "e_ready")
        )
        block_done, zeros, abs_ready = m.sem("block_done"), m.sem("zeros"), m.sem("abs_ready")

        with nc.Block() as block:

            @block.sync
            def _(sp):
                norm.load(nc, sp, io, mod_dram, 1)
                for dst, src in (
                    (cw[:], io["conv_wT"]), (cb[:], io["conv_bT"]), (lam[:], io["rg_lambdaT"]),
                    (ba[:], io["rg_baT"]), (bx[:], io["rg_bxT"]),
                ):
                    sp.dma_start(dst, src).then_inc(small_in, 16)
                w = io["rg_w_in"][0].rearrange("(c p) n -> p c n", p=P)
                for b in range(RB):
                    c0 = DR + b * P
                    if b >= RING:
                        sp.wait_ge(block_done, b - RING + 1)
                    sp.dma_start(W[:, b % RING, :, :], w[:, :, c0 : c0 + P]).then_inc(w_in[b % RING], 16)
                sp.dma_start(wg[:], io["rg_gatesT"]).then_inc(late_in, 16)
                sp.dma_start(g1[:], mod_dram[1, 1, 2].partition_broadcast(P)).then_inc(late_in, 16)
                sp.wait_ge(late_in, 32)

            @block.scalar
            def _(act):
                norm.scalar_sums(nc, act, lambda e, t: None)
                norm.scalar_out(nc, act)
                act.wait_ge(abs_ready, 1)
                nc.scalar.activation(e1[:], z[:], ACT.Exp, scale=-1.0).then_inc(e_ready, 1)
                act.wait_ge(zeros, 1)
                for b in range(RB):
                    if b >= 2:
                        act.wait_ge(conv_done, b - 1)
                    for part, (r0, n) in enumerate(((RAW_CTX, CTX), (RAW_LAT, SEQ))):
                        job = 2 * b + part
                        act.wait_ge(mm_ready, job + 1)
                        nc.scalar.copy(raw[:, b % 2, r0 : r0 + n], MM[:, job % 4, 0:n]).then_inc(mm_free, 1)

            @block.vector
            def _(dve):
                st = Steps(dve, dve_step)
                nc.vector.memset(raw[:], 0.0).then_inc(zeros, 1)
                norm.vector(nc, dve, st)
                dve.wait_ge(small_in, 16 * 5)
                st.then(nc.vector.tensor_scalar(z[:], lam[:], -1.0, None, ALU.mult))
                st.then(nc.vector.tensor_tensor(z[:], z[:], lam[:], ALU.max))
                dve.sem_inc(abs_ready, 1)
                dve.wait_ge(e_ready, 1)
                st.then(nc.vector.tensor_scalar(z2[:], e1[:], 2.0, None, ALU.add))
                st.then(nc.vector.reciprocal(z2[:], z2[:]))
                st.then(nc.vector.tensor_tensor(z[:], e1[:], z2[:], ALU.mult))
                st.then(nc.vector.tensor_tensor(z2[:], z[:], z[:], ALU.mult))
                st.then(nc.vector.memset(poly[:], 1.0 / 17.0))
                for k in range(7, -1, -1):
                    st.then(nc.vector.tensor_tensor(poly[:], poly[:], z2[:], ALU.mult))
                    st.then(nc.vector.tensor_scalar(poly[:], poly[:], 1.0 / (2 * k + 1), None, ALU.add))
                st.then(nc.vector.tensor_tensor(poly[:], poly[:], z[:], ALU.mult))
                st.then(nc.vector.tensor_scalar(e1[:], lam[:], -1.0, 0.0, ALU.mult, ALU.max))
                st.then(
                    nc.vector.scalar_tensor_tensor(out=z[:], in0=poly[:], scalar=2.0, in1=e1[:], op0=ALU.mult, op1=ALU.add)
                )
                st.did(nc.vector.tensor_scalar(cl[:], z[:], -4.0, None, ALU.mult))
                st.then(nc.vector.tensor_scalar(cl2[:], z[:], -8.0, None, ALU.mult))
                for b in range(RB):
                    y, x = XC[:, b, :], raw[:, b % 2, :]
                    dve.wait_ge(mm_free, 2 * b + 2)
                    dve.wait_ge(zeros, 1)
                    st.then(nc.vector.tensor_scalar(y, x[:, 0:XCW], cw[:, b, 0:1], cb[:, b : b + 1], ALU.mult, ALU.add))
                    for j in range(1, CONV):
                        ins = nc.vector.scalar_tensor_tensor(
                            out=y, in0=x[:, j : j + XCW], scalar=cw[:, b, j : j + 1], in1=y, op0=ALU.mult, op1=ALU.add
                        )
                        if j < CONV - 1:
                            st.then(ins)
                    ins.then_inc(conv_done, 1)

            @block.tensor
            def _(pe):
                norm.tensor(nc, pe)
                pe.wait_ge(norm.hT_ready, 2 * NT)
                for b in range(RB):
                    pe.wait_ge(w_in[b % RING], 16 * (b // RING + 1))
                    for part, (a0, a1) in enumerate(((0, CTX), (CTX, TOK))):
                        job = 2 * b + part
                        if job >= 4:
                            pe.wait_ge(mm_free, job - 3)
                        for k in range(DC):
                            ins = nc.tensor.matmul(
                                MM[:, job % 4, 0 : a1 - a0], W[:, b % RING, k, :], hT[:, k, a0:a1],
                                start=(k == 0), stop=(k == DC - 1),
                            )
                        ins.then_inc(mm_ready, 1)
                    pe.wait_ge(mm_ready, job + 1)
                    pe.sem_inc(block_done, 1)


def rg_scan_part(nc, io, X, hT, XC, G, wg, g1, cl, cl2, ba, bx):
    NBG = 5
    NGROUP = RB // NBG
    with ExitStack() as ctx:
        m = Pool(nc, ctx, "rgs")
        A = m.sb("A", [P, NBG, XCW])
        big = m.sb("big", [P, 2, NBG, XCW])
        Mm, IX = big[:, 0, :, :], big[:, 1, :, :]
        scan_ctx = m.sb("scan_ctx", [P, 2, CTX])
        back = m.sb("back", [P, 2, SEQ])
        HF = m.sb("HF", [P, NBG, SEQ])
        W_left = hT[:].rearrange("p c t -> p (c t)")[:, 0 : RB * 512].rearrange("p (k n) -> p k n", k=RB)
        W_right = big[:].rearrange("p a i t -> p (a i t)")[:, 0 : RB * 512].rearrange("p (k n) -> p k n", k=RB)
        WG_RING = 3
        WG = m.sb("WG", [P, WG_RING, DC, P])
        ps, psG = m.ps("ps", [P, 3, 2, 512]), m.ps("psG", [P, 2, 512])
        out_banks = [ps[:, 0, 0, :], ps[:, 1, 0, :], ps[:, 2, 0, :], psG[:, 0, :]]
        wg_in = [m.sem(f"wg_in{r}") for r in range(WG_RING)]
        gate_ready, gelu_done = m.sem("gate_ready"), m.sem("gelu_done")
        ri_ready, ri_taken, th_ready, a_ready, gx_ready, in_ready, sqrt_ready, scanned = (
            m.sem(x)
            for x in ("ri_ready", "ri_taken", "th_ready", "a_ready", "gx_ready", "in_ready", "sqrt_ready", "scanned")
        )
        y_done, out_ready, x_done, dve_step = (m.sem(x) for x in ("y_done", "out_ready", "x_done", "dve_step"))
        w_in = [m.sem(f"w_in{h}") for h in range(2)]
        units = [(g * NBG + i, d) for g in range(NGROUP) for d in range(2) for i in range(NBG)]

        with nc.Block() as block:

            @block.sync
            def _(sp):
                w = io["rg_w_in"][0].rearrange("(c p) n -> p c n", p=P)
                for b in range(RB):
                    if b >= WG_RING:
                        sp.wait_ge(gate_ready, b - WG_RING + 1)
                    sp.dma_start(WG[:, b % WG_RING, :, :], w[:, :, b * P : (b + 1) * P]).then_inc(wg_in[b % WG_RING], 16)
                w = io["rg_w_out"][0].rearrange("(c p) n -> p c n", p=P)
                sp.wait_ge(gate_ready, RB)
                sp.dma_start(W_left, w[:, :, 0:512]).then_inc(w_in[0], 16)
                sp.wait_ge(scanned, len(units))
                sp.dma_start(W_right, w[:, :, 512:1024]).then_inc(w_in[1], 16)

            @block.tensor
            def _(pe):
                def project_gate(b):
                    pe.wait_ge(wg_in[b % WG_RING], 16 * (b // WG_RING + 1))
                    if b >= 2:
                        pe.wait_ge(gelu_done, b - 1)
                    for k in range(DC):
                        ins = nc.tensor.matmul(
                            psG[:, b % 2, :], WG[:, b % WG_RING, k, :], hT[:, k, CTX:TOK], start=(k == 0), stop=(k == DC - 1)
                        )
                    ins.then_inc(gate_ready, 1)

                for b in range(2):
                    project_gate(b)
                for u, (b, d) in enumerate(units):
                    for k in range(2):
                        job = 2 * u + k
                        if job >= 3:
                            pe.wait_ge(ri_taken, job - 2)
                        for h in range(2):
                            ins = nc.tensor.matmul(
                                ps[:, job % 3, h, 0:HALF], wg[:, 2 * k + d, b, :], XC[:, b, h * HALF : (h + 1) * HALF],
                                start=True, stop=True,
                            )
                        ins.then_inc(ri_ready, 1)
                    if u % NBG == NBG - 1:
                        for b in range(2 * (u // NBG) + 2, 2 * (u // NBG) + 4):
                            project_gate(b)
                pe.wait_ge(y_done, RB)
                pe.wait_ge(ri_taken, 2 * len(units))
                for h in range(2):
                    pe.wait_ge(w_in[h], 16)
                    for t in range(LT):
                        n = h * LT + t
                        if n >= 4:
                            pe.wait_ge(x_done, n - 3)
                        for k in range(RB):
                            ins = nc.tensor.matmul(
                                out_banks[n % 4], G[:, k, t * P : (t + 1) * P], (W_left if h == 0 else W_right)[:, k, :],
                                start=(k == 0), stop=(k == RB - 1),
                            )
                        ins.then_inc(out_ready, 1)

            @block.scalar
            def _(act):
                def gelu_pair(q):
                    for b in (2 * q, 2 * q + 1):
                        act.wait_ge(gate_ready, b + 1)
                        nc.scalar.activation(G[:, b, :], psG[:, b % 2, :], ACT.Gelu_apprx_tanh).then_inc(gelu_done, 1)

                for g0 in range(0, len(units), NBG):
                    gelu_pair(g0 // NBG)
                    for i in range(NBG):
                        u = g0 + i
                        b, d = units[u]
                        act.wait_ge(ri_ready, 2 * u + 1)
                        if u >= NBG:
                            act.wait_ge(scanned, u - NBG + 1)
                        nc.scalar.activation(
                            A[:, i, :].rearrange("p (a k) -> p a k", a=2), ps[:, 2 * u % 3, :, 0:HALF], ACT.Sigmoid,
                            bias=ba[:, d, b : b + 1],
                        ).then_inc(ri_taken, 1)
                        act.wait_ge(ri_ready, 2 * u + 2)
                        nc.scalar.activation(
                            IX[:, i, :].rearrange("p (a k) -> p a k", a=2), ps[:, (2 * u + 1) % 3, :, 0:HALF], ACT.Sigmoid,
                            bias=bx[:, d, b : b + 1],
                        ).then_inc(ri_taken, 1)
                        act.wait_ge(ri_taken, 2 * u + 1)
                        nc.scalar.activation(Mm[:, i, :], A[:, i, :], ACT.Tanh, scale=cl[:, d, b : b + 1]).then_inc(
                            th_ready, 1
                        )
                    for i in range(NBG):
                        b, d = units[g0 + i]
                        act.wait_ge(th_ready, g0 + i + 1)
                        nc.scalar.activation(A[:, i, :], A[:, i, :], ACT.Exp, scale=cl2[:, d, b : b + 1]).then_inc(a_ready, 1)
                    for i in range(NBG):
                        nc.scalar.activation(Mm[:, i, :], Mm[:, i, :], ACT.Sqrt, scale=-1.0).then_inc(sqrt_ready, 1)
                gelu_pair(len(units) // NBG)

            @block.gpsimd
            def _(pool):
                for g0 in range(0, len(units), NBG):
                    for i in range(NBG):
                        b, d = units[g0 + i]
                        pool.wait_ge(ri_taken, 2 * (g0 + i) + 2)
                        nc.gpsimd.tensor_tensor(IX[:, i, :], IX[:, i, :], XC[:, b, :], ALU.mult).then_inc(gx_ready, 1)
                    for i in range(NBG):
                        pool.wait_ge(gx_ready, g0 + i + 1)
                        pool.wait_ge(sqrt_ready, g0 + i + 1)
                        nc.gpsimd.tensor_tensor(IX[:, i, :], IX[:, i, :], Mm[:, i, :], ALU.mult).then_inc(in_ready, 1)

            @block.vector
            def _(dve):
                st = Steps(dve, dve_step)

                def scan(u):
                    b, d = units[u]
                    i = u % NBG
                    dve.wait_ge(a_ready, u + 1)
                    dve.wait_ge(in_ready, u + 1)
                    st.then(
                        nc.vector.scalar_tensor_tensor(
                            out=Mm[:, i, :], in0=A[:, i, :], scalar=1.0, in1=IX[:, i, :], op0=ALU.add, op1=ALU.mult
                        )
                    )
                    c, lat = slice(OUT_CTX, OUT_CTX + CTX), slice(OUT_LAT, OUT_LAT + SEQ)
                    ac, uc, al, ul = A[:, i, c], Mm[:, i, c], A[:, i, lat], Mm[:, i, lat]
                    sc, out = scan_ctx[:, u % 2, :], HF[:, i, :] if d == 0 else back[:, u % 2, :]
                    if d == 0:
                        st.then(nc.vector.tensor_tensor_scan(sc, ac, uc, 0.0, ALU.mult, ALU.add))
                        ins = nc.vector.tensor_tensor_scan(out, al, ul, sc[:, CTX - 1 : CTX], ALU.mult, ALU.add)
                    else:
                        st.then(nc.vector.tensor_tensor_scan(sc[:, ::-1], ac[:, ::-1], uc[:, ::-1], 0.0, ALU.mult, ALU.add))
                        ins = nc.vector.tensor_tensor_scan(
                            out[:, ::-1], al[:, ::-1], ul[:, ::-1], sc[:, 0:1], ALU.mult, ALU.add
                        )
                    ins.then_inc(scanned, 1)
                    if d == 1:
                        dve.wait_ge(scanned, u + 1)
                        st.then(nc.vector.tensor_tensor(out, out, HF[:, i, :], ALU.add))
                        dve.wait_ge(gelu_done, b + 1)
                        nc.vector.tensor_tensor(G[:, b, :], G[:, b, :], out, ALU.mult).then_inc(y_done, 1)

                for u in range(len(units)):
                    scan(u)
                tmp = scan_ctx[:].rearrange("p a b -> p (a b)")
                for n in range(2 * LT):
                    h, t = n // LT, n % LT
                    cols = slice(512 * h, 512 * h + 512)
                    dve.wait_ge(out_ready, n + 1)
                    if n:
                        dve.wait_ge(x_done, n)
                    st.then(nc.vector.tensor_tensor(tmp, out_banks[n % 4], g1[:, cols], ALU.mult))
                    x = X[:, CT + t, cols]
                    nc.vector.tensor_tensor(x, x, tmp, ALU.add).then_inc(x_done, 1)




def constants():
    n = np.arange(SEQ)
    freq = (10000.0 ** (-np.arange(HD // 4, dtype=np.float32) / (HD // 4))).astype(np.float32)
    ang = np.stack([(n // GRID_W).astype(np.float32)[:, None] * freq, (n % GRID_W).astype(np.float32)[:, None] * freq], 1)
    cos = np.ones((HD, TOK), np.float32)
    sin = np.zeros((HD, TOK), np.float32)
    rot = np.zeros((HD, HD), np.float32)
    f = HD // 4
    for axis in range(2):
        for half in range(2):
            a = axis * 2 * f + half * f
            cos[a : a + f, CTX:] = np.cos(ang[:, axis]).T
            sin[a : a + f, CTX:] = np.sin(ang[:, axis]).T
            b = axis * 2 * f + (1 - half) * f
            rot[b + np.arange(f), a + np.arange(f)] = -1.0 if half == 0 else 1.0
    return {
        "cos": cos, "sin": sin, "rotm": rot, "ident": np.eye(P, dtype=np.float32),
        "iota": np.tile(np.arange(TOPK, dtype=np.float32), (P, 1)),
    }


def constants_stage(nc, io, ident, ones, eps):
    with ExitStack() as ctx:
        m = Pool(nc, ctx, "const")
        const_in = m.sem("const_in")
        with nc.Block() as block:

            @block.sync
            def _(sp):
                sp.dma_start(ident[:], io["ident"]).then_inc(const_in, 16)
                sp.wait_ge(const_in, 16)

            @block.vector
            def _(dve):
                nc.vector.memset(ones[:], 1.0)
                nc.vector.memset(eps[:], EPS)


def trunk(nc, io, out):
    mod_dram = nc.dram_tensor("modulation", (2, 2, 6, D), F32, kind="Internal").ap()
    with ExitStack() as ctx:
        m = Pool(nc, ctx, "all")
        ident, ones, eps = m.sb("ident", [P, P]), m.sb("ones", [P, P]), m.sb("eps", [P, 1])
        constants_stage(nc, io, ident, ones, eps)
        X = m.sb("X", [P, NT, D])
        with ExitStack() as x_load:
            m_x = Pool(nc, x_load, "x_load")
            x_in = [m_x.sem(f"x_in{t}") for t in range(NT)]
            modulation_stage(nc, io, mod_dram, X, x_in)
            mixer_ab_stage(nc, io, mod_dram, X, x_in, ident, ones, eps)
        peer_stage(nc, io, mod_dram, X, ident, eps, 0, 0, None)
        mixer_rg_stage(nc, io, mod_dram, X, ident, eps)
        peer_stage(nc, io, mod_dram, X, ident, eps, 1, CT, out)


def layouts(inp):
    f = lambda a: np.ascontiguousarray(a)
    io = {
        n: f(inp[n])
        for n in (
            "x", "c", "ctx", "c_ctx", "mod_w", "mod_b", "norm1_g", "norm2_g", "ab_w_in", "gmlp_bs", "ab_w_out",
            "rg_w_in", "rg_w_out", "peer_wq", "final_norm_g",
        )
    }
    io["wsT"] = f(inp["gmlp_ws"][0].transpose(2, 0, 1))
    io["gmlp_gT"] = f(inp["gmlp_norm_g"][0].reshape(GROUPS, P).T)
    io["qk_gT"] = f(np.stack([inp["q_norm_g"][0], inp["k_norm_g"][0]], 1))
    for layer in range(2):
        io[f"peer_u{layer}"] = f(inp["peer_u"][layer])
        io[f"peer_v{layer}"] = f(inp["peer_v"][layer])
    io["keysT"] = f(inp["peer_keys"].transpose(0, 4, 1, 2, 3).reshape(2, P, 2 * HEADS, KEYS))
    io["conv_wT"] = f(inp["rg_conv_w"][0].reshape(CONV, RB, P).transpose(2, 1, 0))
    io["conv_bT"] = f(inp["rg_conv_b"][0].reshape(RB, P).T)
    gates = np.concatenate([inp["rg_wa"][0], inp["rg_wx"][0]])
    io["rg_gatesT"] = f(gates.transpose(2, 0, 1, 3))
    for n in ("rg_ba", "rg_bx", "rg_lambda"):
        io[n + "T"] = f(inp[n][0].reshape(2, RB, P).transpose(2, 0, 1))
    io.update(constants())
    return io


def kernel(**inputs):
    import concourse.bacc as bacc
    from concourse.bass_utils import run_bass_kernel_spmd

    arrays = layouts({n: np.asarray(a) for n, a in inputs.items()})
    nc = bacc.Bacc("TRN2", target_bir_lowering=False, num_devices=1)
    io = {
        n: nc.dram_tensor("in_" + n, a.shape, mybir.dt.from_np(a.dtype), kind="ExternalInput").ap()
        for n, a in arrays.items()
    }
    out = nc.dram_tensor("out", (1, SEQ, D), F32, kind="ExternalOutput").ap()
    trunk(nc, io, out)
    got = run_bass_kernel_spmd(nc, [{"in_" + n: a for n, a in arrays.items()}], core_ids=[0])
    return got.results[0]["out"]
```
